# Optimizing a Trainium2 kernel written in Bass

```python
import math
import jax, jax.numpy as jnp
from jax import lax
import numpy as np

D_MODEL = 2048
BATCH = 1
SEQ = 512
DEPTH = 2
DEC_BATCH = 8
DEC_SEQ = 16
PAST_LEN = 128

CHUNK = 64
PLE_DIM = 256
POOL_W = 1024
POOL_WINDOWS = (2, 4, 8, 16)
POOL_GROUPS = len(POOL_WINDOWS)
POOL_GW = POOL_W // POOL_GROUPS
POOL_HIST = max(POOL_WINDOWS) - 1
RET_HEADS = 4
RET_DK = 256
RET_DV = 256
RET_W = RET_HEADS * RET_DV
MIX_W = POOL_W + RET_W
IN_W = 2 * POOL_W + 2 * RET_HEADS * RET_DK + 2 * RET_W
ROPE_BASE = 10000.0
EPS = 1e-6
GN_EPS = 1e-5

kernel_name = 'hymba_pool_retnet_streaming_step'

def rmsnorm(x, g):
    x32 = x.astype(jnp.float32)
    y = x32 * lax.rsqrt(jnp.mean(x32 * x32, axis=-1, keepdims=True) + EPS)
    return (y * g.astype(jnp.float32)).astype(x.dtype)

def rotary(x, pos):
    half = x.shape[-1] // 2
    inv = 1.0 / (ROPE_BASE ** (jnp.arange(half, dtype=jnp.float32) / half))
    ang = pos[:, None] * inv[None, :]
    cos = jnp.cos(ang)[None, :, None, :]
    sin = jnp.sin(ang)[None, :, None, :]
    x32 = x.astype(jnp.float32)
    x1, x2 = x32[..., :half], x32[..., half:]
    return jnp.concatenate([x1 * cos - x2 * sin, x1 * sin + x2 * cos], axis=-1)

def pool_mix(u, hist, offset, w_pool, pool_scale):
    B, L, _ = u.shape
    u32 = u.astype(jnp.float32)
    z = jnp.concatenate([hist.astype(jnp.float32), u32], axis=1)
    cs = jnp.concatenate([jnp.zeros((B, 1, POOL_W), jnp.float32),
                          jnp.cumsum(z, axis=1)], axis=1)
    pos = (offset + jnp.arange(L)).astype(jnp.float32)
    outs = []
    for g, w in enumerate(POOL_WINDOWS):
        sl = slice(g * POOL_GW, (g + 1) * POOL_GW)
        s = cs[:, POOL_HIST + 1:POOL_HIST + 1 + L, sl] - cs[:, POOL_HIST + 1 - w:POOL_HIST + 1 - w + L, sl]
        cnt = jnp.minimum(jnp.float32(w), pos + 1.0)
        outs.append(s / cnt[None, :, None])
    pooled = jnp.concatenate(outs, axis=-1) - u32
    pooled = pooled.reshape(B, L, POOL_GROUPS, POOL_GW)
    y = jnp.einsum('blgc,gcd->blgd', pooled, w_pool.astype(jnp.float32)).reshape(B, L, POOL_W)
    y = y * pool_scale.astype(jnp.float32)
    new_hist = z[:, -POOL_HIST:, :].astype(hist.dtype)
    return y, new_hist

def retention(q, k, v, S0):
    B, L, H, _ = q.shape
    C = min(CHUNK, L)
    nC = L // C
    lg = jnp.log(1.0 - 2.0 ** (-5.0 - jnp.arange(H, dtype=jnp.float32)))
    idx = jnp.arange(C, dtype=jnp.float32)
    diff = idx[:, None] - idx[None, :]
    D = jnp.where(diff[None] >= 0, jnp.exp(jnp.maximum(diff, 0.0)[None] * lg[:, None, None]), 0.0)
    q_decay = jnp.exp((idx[None, :] + 1.0) * lg[:, None])
    k_decay = jnp.exp((C - 1.0 - idx[None, :]) * lg[:, None])
    chunk_decay = jnp.exp(C * lg)

    def to_chunks(t):
        return t.reshape(B, nC, C, H, t.shape[-1]).transpose(1, 0, 3, 2, 4)

    qs, ks, vs = to_chunks(q), to_chunks(k), to_chunks(v.astype(jnp.float32))

    def step(S, inp):
        qc, kc, vc = inp
        scores = jnp.einsum('bhnd,bhmd->bhnm', qc, kc) * D[None]
        o_in = jnp.einsum('bhnm,bhmv->bhnv', scores, vc)
        o_x = jnp.einsum('bhnd,bhdv->bhnv', qc * q_decay[None, :, :, None], S)
        S_new = S * chunk_decay[None, :, None, None] + jnp.einsum(
            'bhmd,bhmv->bhdv', kc * k_decay[None, :, :, None], vc)
        return S_new, o_in + o_x

    S_fin, o = lax.scan(step, S0.astype(jnp.float32), (qs, ks, vs))
    o = o.transpose(1, 0, 3, 2, 4).reshape(B, L, H, RET_DV)
    return o, S_fin.astype(S0.dtype)

def layer(h, p_i, hist, S0, offset, g_mix, w_in, w_pool, pool_scale, g_gn, w_out, g_ple, w_pg, w_ple):
    B, L, _ = h.shape
    hn = rmsnorm(h, g_mix)
    z = hn @ w_in
    u, gp, q, k, v, gr = jnp.split(z, 6, axis=-1)
    y_pool, new_hist = pool_mix(u, hist, offset, w_pool, pool_scale)
    y_pool = y_pool * jax.nn.silu(gp.astype(jnp.float32))
    pos = (offset + jnp.arange(L)).astype(jnp.float32)
    qr = rotary(q.reshape(B, L, RET_HEADS, RET_DK), pos)
    kr = rotary(k.reshape(B, L, RET_HEADS, RET_DK), pos) * (RET_DK ** -0.5)
    o, S_new = retention(qr, kr, v.reshape(B, L, RET_HEADS, RET_DV), S0)
    mu = jnp.mean(o, axis=-1, keepdims=True)
    var = jnp.mean(jnp.square(o - mu), axis=-1, keepdims=True)
    o = ((o - mu) * lax.rsqrt(var + GN_EPS)).reshape(B, L, RET_W) * g_gn.astype(jnp.float32)
    o = o * jax.nn.silu(gr.astype(jnp.float32))
    mix = jnp.concatenate([y_pool, o], axis=-1).astype(h.dtype)
    h = h + mix @ w_out
    gate = jax.nn.sigmoid((rmsnorm(h, g_ple) @ w_pg).astype(jnp.float32))
    h = h + (gate * (p_i @ w_ple).astype(jnp.float32)).astype(h.dtype)
    return h, new_hist, S_new

def trunk(x, p, hist0, S0, offset, g_mix, w_in, w_pool, pool_scale, g_gn, w_out, g_ple, w_pg, w_ple, g_final):
    h = x
    hists, states = [], []
    for i in range(DEPTH):
        h, nh, ns = layer(h, p[i], hist0[i], S0[i], offset, g_mix[i], w_in[i], w_pool[i],
                          pool_scale[i], g_gn[i], w_out[i], g_ple[i], w_pg[i], w_ple[i])
        hists.append(nh)
        states.append(ns)
    return rmsnorm(h, g_final), jnp.stack(hists, axis=0), jnp.stack(states, axis=0)

def setup_inputs(seed: int = 0) -> dict:
    key = jax.random.key(seed)
    ks = jax.random.split(key, 20)
    f32 = jnp.float32
    nrm = lambda k, s, sc: jax.random.normal(k, s, f32) * sc
    return {
        'x_prompt': nrm(ks[0], (BATCH, SEQ, D_MODEL), 1.0),
        'x_sample': nrm(ks[1], (DEC_BATCH, DEC_SEQ, D_MODEL), 1.0),
        'p_prompt': nrm(ks[2], (DEPTH, BATCH, SEQ, PLE_DIM), 1.0),
        'p_sample': nrm(ks[3], (DEPTH, DEC_BATCH, DEC_SEQ, PLE_DIM), 1.0),
        'state_pool': nrm(ks[4], (DEPTH, DEC_BATCH, POOL_HIST, POOL_W), 1.0),
        'state_ret': nrm(ks[5], (DEPTH, DEC_BATCH, RET_HEADS, RET_DK, RET_DV), 0.1),
        'g_mix': 1.0 + nrm(ks[6], (DEPTH, D_MODEL), 0.02),
        'w_in': nrm(ks[7], (DEPTH, D_MODEL, IN_W), D_MODEL ** -0.5),
        'w_pool': nrm(ks[8], (DEPTH, POOL_GROUPS, POOL_GW, POOL_GW), POOL_GW ** -0.5),
        'pool_scale': 1.0 + nrm(ks[9], (DEPTH, POOL_W), 0.02),
        'g_gn': 1.0 + nrm(ks[10], (DEPTH, RET_W), 0.02),
        'w_out': nrm(ks[11], (DEPTH, MIX_W, D_MODEL), MIX_W ** -0.5),
        'g_ple': 1.0 + nrm(ks[12], (DEPTH, D_MODEL), 0.02),
        'w_pg': nrm(ks[13], (DEPTH, D_MODEL, D_MODEL), D_MODEL ** -0.5),
        'w_ple': nrm(ks[14], (DEPTH, PLE_DIM, D_MODEL), PLE_DIM ** -0.5),
        'g_final': 1.0 + nrm(ks[15], (D_MODEL,), 0.02),
    }

def reference(x_prompt, x_sample, p_prompt, p_sample, state_pool, state_ret, g_mix, w_in, w_pool,
              pool_scale, g_gn, w_out, g_ple, w_pg, w_ple, g_final):
    hist0 = jnp.zeros((DEPTH, BATCH, POOL_HIST, POOL_W), x_prompt.dtype)
    S0 = jnp.zeros((DEPTH, BATCH, RET_HEADS, RET_DK, RET_DV), x_prompt.dtype)
    y_prompt, new_pool_prompt, new_ret_prompt = trunk(
        x_prompt, p_prompt, hist0, S0, 0, g_mix, w_in, w_pool, pool_scale, g_gn, w_out,
        g_ple, w_pg, w_ple, g_final)
    y_sample, new_pool_sample, new_ret_sample = trunk(
        x_sample, p_sample, state_pool, state_ret, PAST_LEN, g_mix, w_in, w_pool, pool_scale,
        g_gn, w_out, g_ple, w_pg, w_ple, g_final)
    return (y_prompt, y_sample, new_pool_prompt, new_ret_prompt, new_pool_sample, new_ret_sample)


_drawn_inputs = setup_inputs


def setup_inputs(seed=0):
    import zlib

    import numpy as np

    out = dict(_drawn_inputs(seed))
    spreads = {}
    factors = {'pool_scale': 6.807, 'g_gn': 6.091, 'g_ple': 8.0, 'g_final': 2.746}
    for name, (base, spread) in spreads.items():
        noise = np.random.default_rng([zlib.crc32(name.encode()), seed]).standard_normal(out[name].shape)
        drawn = base * np.exp(spread * noise) if base else spread * noise
        out[name] = __import__('jax').numpy.asarray(drawn.astype(out[name].dtype))
    for name, factor in factors.items():
        out[name] = (out[name] * factor).astype(out[name].dtype)
    return out
```

```python
from contextlib import ExitStack

import concourse.bass as bass
from concourse import mybir

F32 = mybir.dt.float32
F32R = mybir.dt.float32r
ALU = mybir.AluOpType
ACT = mybir.ActivationFunctionType

P = 128
D = 2048
DEPTH = 2
NT = 5
TOK = NT * P
NPT = 4
SB, SL = 8, 16
HEADS = 4
DH = 256
HIST = 15
WINDOWS = (2, 4, 8, 16)
PAST = 128
PLE = 256
NW = 512
KT = D // P
PAIRS = KT // 2
EPS, GN_EPS = 1e-6, 1e-5

G_HEAD = 3
G_OUT = D // NW
G_LAYER = HEADS * G_HEAD + 2 * G_OUT
M_LAYER = G_LAYER * PAIRS

T_UNITS = 20
H_UNITS = 30
PT_UNITS = 4
PLE_UNITS = 6
S_PRO = 0
S_HEAD = S_PRO + T_UNITS
S_OUT = S_HEAD + HEADS * H_UNITS
S_PG0 = S_OUT + T_UNITS + PT_UNITS
S_PG = S_PG0 + T_UNITS + PLE_UNITS
S_LAYER = S_PG + (G_OUT - 1) * PLE_UNITS
U_BAND, U_MAP, U_QT, U_KT, U_SC = 0, 3, 6, 9, 12
U_O = (14, 20, 22, 24)
U_D = (15, 21, 23, 25)
U_DS = (16, 17, 18, 19, 26, 27, 28, 29)
STAGES = NT * (HEADS + 2 * G_OUT)

C_MASKP, C_MASKS, C_BAND0, C_BAND, C_PREV, C_BANDS, C_HISTS = (i * P for i in range(7))
C_D = 7 * P
C_D2 = C_D + NT
C_VP = C_D2 + NT
C_GP, C_GS = C_VP + 1, C_VP + 2
C_VS = C_GS + 1
C_HEAD = C_VS + SB + 3

PC_MIX, PC_OUT, PC_PLE, PC_LAYER = 0, KT, 2 * KT, 3 * KT

T_BATCH = []
for _j in range(PAIRS):
    _q = _j // 2
    T_BATCH.append(([("s", _q)] if _j % 2 == 0 else []) + [("p", 2 * _j), ("p", 2 * _j + 1)])
T_FIRST = [sum(len(b) for b in T_BATCH[:j]) for j in range(PAIRS + 1)]


def build(nc, a):
    with ExitStack() as ctx:
        def sb(name, shape, dt=F32):
            return ctx.enter_context(nc.sbuf_tensor(name, shape, dt))

        def psum(name, shape):
            return ctx.enter_context(nc.psum_tensor(name, shape, F32))

        def sem(name):
            return ctx.enter_context(nc.semaphore(name))

        H = sb("H", [P, NT, D])
        Ahi = sb("Ahi", [P, KT, TOK], F32R)
        Alo = sb("Alo", [P, KT, TOK], F32R)
        raw = sb("raw", [P, 2, 2, NW])
        Whi = sb("Whi", [P, 2, 2, NW], F32R)
        Wlo = sb("Wlo", [P, 2, 2, NW], F32R)
        Z = sb("Z", [P, NT, NW])
        qT = sb("qT", [P, 2, TOK])
        kT = sb("kT", [P, 2, TOK])
        ST = sb("ST", [P, NT, P])
        Sp = sb("Sp", [P, 2, DH])
        vd = sb("vd", [P, 2, DH])
        vdm = sb("vdm", [P, 2, DH])
        qTm = sb("qTm", [P, 2, SB, P])
        Ss = sb("Ss", [P, 4, 2, DH])
        head = sb("head", [P, C_HEAD])
        wpool = sb("wpool", [P, 2, DH])
        hist = sb("hist", [P, DH])
        rope = sb("rope", [P, NT, DH])
        stage = sb("stage", [P, 2, NW])
        tA = sb("tA", [P, 2, P])
        tB = sb("tB", [P, 2, P])
        ident = sb("ident", [P, P])
        par = sb("par", [P, DEPTH * PC_LAYER])
        parl = sb("parl", [P, PC_LAYER])
        ssq = sb("ssq", [P, NT, 2])
        ms = sb("ms", [P, NT])
        rstd = sb("rstd", [P, NT])
        mhalf = sb("mhalf", [P, NT])
        st6 = sb("st6", [P, NT, 6])
        mv = sb("mv", [P, NT, 2])
        gv = sb("gv", [P, NT])
        gp = sb("gp", [P, NT])
        gr = sb("gr", [P, NT])

        pooledT, P5, pT = kT, kT[:].rearrange("p a b -> p (a b)").rearrange("p (t c) -> p t c", t=NT), qT
        wple = Ss[:, 0:2].rearrange("p a b c -> p (a b c)").rearrange("p (k n) -> p k n", k=2)
        gfin = Z[:].rearrange("p t n -> p (t n)")[:, 0:D]
        pstage = stage[0:DEPTH * PC_LAYER, 0, 0:P]

        acc = psum("acc", [P, NT, NW])
        side = psum("side", [P, 2, NW])
        osb = psum("osb", [P, NW])

        hres = nc.dram_tensor("h_residual", [TOK, D], F32, kind="Internal").ap()

        settled = sem("settled")
        const_in = sem("const_in")
        par_t, par_c, parl_c, zeroed = sem("par_t"), sem("par_c"), sem("parl_c"), sem("zeroed")
        h_in = sem("h_in")
        w_landed = [sem("w_landed0"), sem("w_landed1")]
        w_hi, w_lo, w_used = sem("w_hi"), sem("w_lo"), sem("w_used")
        acc_ready = sem("acc_ready")
        acc_out = sem("acc_out")
        side_ready, side_free = sem("side_ready"), sem("side_free")
        t_hi = sem("t_hi")
        sq_done, ms_done, rstd_done, rstd_ok = sem("sq_done"), sem("ms_done"), sem("rstd_done"), sem("rstd_ok")
        rot_done = sem("rot_done")
        head_in = sem("head_in")
        upool_out = sem("upool_out")
        s_in = [sem(f"s_in{j}") for j in range(4)]
        s_out = [sem(f"s_out{j}") for j in range(4)]
        sp_out = sem("sp_out")
        qtm_in, vd_in, vdm_in = sem("qtm_in"), sem("vd_in"), sem("vdm_in")
        os_ready, os_free = sem("os_ready"), sem("os_free")
        gn_in, gn_pow = sem("gn_in"), sem("gn_pow")
        stage_free = sem("stage_free")
        hres_out, res_in = sem("hres_out"), sem("res_in")
        p_in, wple_in = sem("p_in"), sem("wple_in")
        ch_rot, ch_gn, ch_gate, ch_ms, ch_pg, ch_fin = (sem(n) for n in
            ("ch_rot", "ch_gn", "ch_gate", "ch_ms", "ch_pg", "ch_fin"))
        gfin_in, y_in, y_out = sem("gfin_in"), sem("y_in"), sem("y_out")

        w_in_v = a["w_in"].rearrange("l (k p) (s c) -> l p k s c", p=P, s=6)
        w_out_v = a["w_out"].rearrange("l (k p) c -> l p k c", p=P)
        w_pg_v = a["w_pg"].rearrange("l (k p) c -> l p k c", p=P)
        w_ple_v = a["w_ple"].rearrange("l (k p) c -> l p k c", p=P)
        w_pool_v = a["w_pool"].rearrange("l g (k p) c -> l g p k c", p=P)
        st_v = a["state_ret"].rearrange("l b h (k p) c -> l b h p k c", p=P)
        nst_v = a["new_ret_sample"].rearrange("l b h (k p) c -> l b h p k c", p=P)
        nsp_v = a["new_ret_prompt"].rearrange("l b h (k p) c -> l b h p k c", p=P)
        hist_v = a["state_pool"].rearrange("l b j c -> l (b j) c")
        hres_v = hres.rearrange("(t p) n -> p t n", p=P)
        one = bass.ds

        block = ctx.enter_context(nc.Block())

        def settle(e):
            e.sem_inc(settled, 1)

        @block.sync
        def _(sp):
            sp.dma_start(H[:, 0:NPT, :], a["x_prompt"].rearrange("b (t p) n -> p (b t) n", p=P)).then_inc(h_in, 16)
            sp.dma_start(H[:, NPT, :], a["x_sample"].rearrange("b s n -> (b s) n")).then_inc(h_in, 16)

            with sp.Fori(0, DEPTH) as l:
                with sp.Fori(0, HEADS) as h:
                    for j, segs in enumerate((slice(0, 3, 2), slice(3, 5), slice(1, 6, 4))):
                        m0 = sp.snap(l * M_LAYER + h * (G_HEAD * PAIRS) + j * PAIRS)
                        for p in range(PAIRS):
                            src = w_in_v[one(l, 1), :, 2 * p:2 * p + 2, segs, one(h * DH, DH)]
                            sp.wait_ge(w_lo, m0 + p + 1)
                            for kk in range(2):
                                sp.dma_start(raw[:, p % 2, kk, :].rearrange("p (s c) -> p s c", s=2),
                                             src[:, :, kk].rearrange("l p s c -> p (l s) c")) \
                                    .then_inc(w_landed[p % 2], 16)
                for base, view in ((HEADS * G_HEAD, w_out_v), (HEADS * G_HEAD + G_OUT, w_pg_v)):
                    with sp.Fori(0, G_OUT) as g:
                        m0 = sp.snap(l * M_LAYER + g * PAIRS + base * PAIRS)
                        for p in range(PAIRS):
                            src = view[one(l, 1), :, 2 * p:2 * p + 2, one(g * NW, NW)]
                            sp.wait_ge(w_lo, m0 + p + 1)
                            for kk in range(2):
                                sp.dma_start(raw[:, p % 2, kk, :], src[:, :, kk].rearrange("l p c -> p (l c)")) \
                                    .then_inc(w_landed[p % 2], 16)

            for t in range(NT):
                sp.wait_ge(y_in, t + 1)
                dst = a["y_prompt"][0, t * P:(t + 1) * P, :] if t < NPT else \
                    a["y_sample"].rearrange("b s n -> (b s) n")
                sp.dma_start(dst, H[:, t, :]).then_inc(y_out, 16)
            sp.wait_ge(y_out, 16 * NT)

        @block.gpsimd
        def _(po):
            po.dma_start(ident[:], a["c_ident"]).then_inc(const_in, 16)
            for l in range(DEPTH):
                r = l * PC_LAYER
                for src, r0, n in ((a["g_mix"], 0, 16), (a["pool_scale"], 16, 8), (a["g_gn"], 24, 8),
                                   (a["g_ple"], 32, 16)):
                    po.dma_start(stage[r + r0:r + r0 + n, 0, 0:P],
                                 src[l, :].rearrange("(k c) -> k c", c=P)).then_inc(const_in, 16)
            for t in range(NT):
                po.dma_start(rope[:, t], a["c_rope"][:, t]).then_inc(s_out[t] if t < 4 else sp_out, 16)
            po.memset(qTm[:], 0.0).then_inc(zeroed, 1)
            po.memset(mhalf[:], -0.5).then_inc(zeroed, 1)
            po.wait_ge(zeroed, 2)

            def rsqrt(n):
                po.wait_ge(ms_done, n)
                settle(po)
                nc.gpsimd.tensor_tensor(rstd[:], ms[:], mhalf[:], ALU.pow).then_inc(rstd_done, 1)

            with po.Fori(0, DEPTH) as l:
                po.wait_ge(h_in, 32)
                po.wait_ge(stage_free, l * STAGES + 2)
                settle(po)
                po.dma_start(hres_v, H[:]).then_inc(hres_out, 16)
                rsqrt(l * 2 + 1)
                with po.Fori(0, HEADS) as h:
                    hh = po.snap(l * HEADS + h)
                    s0 = po.snap(l * S_LAYER + h * H_UNITS + S_HEAD)
                    po.wait_ge(stage_free, l * STAGES + h * NT + 2)
                    settle(po)
                    po.dma_start(head[:], a["c_head"][one(h, 1)].rearrange("o p c -> p (o c)")).then_inc(head_in, 16)
                    po.dma_start(wpool[:], w_pool_v[one(l, 1), one(h, 1)].rearrange("l g p k c -> p (l g k) c")) \
                        .then_inc(head_in, 16)
                    po.dma_start(hist[0:SB * HIST, :], hist_v[one(l, 1), :, one(h * DH, DH)]
                                 .rearrange("l r c -> r (l c)")).then_inc(head_in, 16)

                    def load_state(b, n):
                        po.wait_ge(s_out[b % 4], (hh * 2 + n) * 16 + 16)
                        settle(po)
                        po.dma_start(Ss[:, b % 4], st_v[one(l, 1), b, one(h, 1)]
                                     .rearrange("l h p k c -> p (l h k) c")).then_inc(s_in[b % 4], 16)

                    def store_state(b):
                        po.wait_ge(side_free, s0 + U_DS[b] + 3)
                        settle(po)
                        po.dma_start(nst_v[one(l, 1), b, one(h, 1)].rearrange("l h p k c -> p (l h k) c"),
                                     Ss[:, b % 4]).then_inc(s_out[b % 4], 16)

                    for b in range(4):
                        load_state(b, 0)
                    po.wait_ge(acc_out, l * (G_LAYER * NT) + h * (G_HEAD * NT) + 2 * NT)
                    settle(po)
                    po.dma_start(a["new_pool_prompt"][one(l, 1), 0, :, one(h * DH, DH)].rearrange("l r c -> r (l c)"),
                                 Z[P - HIST:P, NPT - 1, 0:DH]).then_inc(upool_out, 16)
                    for b in range(SB):
                        po.dma_start(a["new_pool_sample"][one(l, 1), b, :, one(h * DH, DH)]
                                     .rearrange("l r c -> r (l c)"),
                                     Z[b * SL + 1:(b + 1) * SL, NPT, 0:DH]).then_inc(upool_out, 16)
                    for b in range(4):
                        store_state(b)
                    for b in range(4, 8):
                        load_state(b, 1)
                    po.wait_ge(side_free, s0 + U_D[3] + 3)
                    settle(po)
                    po.dma_start(nsp_v[one(l, 1), 0, one(h, 1)].rearrange("l h p k c -> p (l h k) c"),
                                 Sp[:]).then_inc(sp_out, 16)
                    for b in range(4, 8):
                        store_state(b)
                    po.wait_ge(gn_in, hh + 1)
                    settle(po)
                    nc.gpsimd.tensor_tensor(gp[:], gv[:], mhalf[:], ALU.pow).then_inc(gn_pow, 1)
                po.wait_ge(side_free, l * S_LAYER + S_OUT + 2)
                settle(po)
                po.dma_start(P5[:, 0:NPT, :], a["p_prompt"][one(l, 1)].rearrange("l b (t p) c -> p (l b t) c", p=P)) \
                    .then_inc(p_in, 16)
                po.dma_start(P5[:, NPT, :], a["p_sample"][one(l, 1)].rearrange("l b s c -> (l b s) c")).then_inc(p_in, 16)
                po.wait_ge(hres_out, l * 16 + 16)
                settle(po)
                with po.Fori(0, G_OUT) as g:
                    po.wait_ge(stage_free, l * STAGES + g * NT + (HEADS * NT + 2))
                    settle(po)
                    po.dma_start(Z[:], hres_v[:, :, one(g * NW, NW)]).then_inc(res_in, 16)
                for j in range(4):
                    po.wait_ge(s_out[j], (l * HEADS + HEADS) * 32 + 16)
                settle(po)
                po.dma_start(wple, w_ple_v[one(l, 1), :, :, 0:NW].rearrange("l p k c -> p (l k) c")).then_inc(wple_in, 16)
                rsqrt(l * 2 + 2)
                with po.Fori(1, G_OUT) as g:
                    po.wait_ge(side_free, l * S_LAYER + g * PLE_UNITS + (S_PG - PLE_UNITS + 2))
                    settle(po)
                    po.dma_start(wple, w_ple_v[one(l, 1), :, :, one(g * NW, NW)].rearrange("l p k c -> p (l k) c")) \
                        .then_inc(wple_in, 16)
            po.wait_ge(stage_free, DEPTH * STAGES + 2)
            po.dma_start(gfin, a["g_final"].partition_broadcast(P)).then_inc(gfin_in, 16)
            rsqrt(2 * DEPTH + 1)
            po.wait_ge(upool_out, DEPTH * HEADS * 16 * (SB + 1))
            for j in range(4):
                po.wait_ge(s_out[j], DEPTH * HEADS * 32 + 16)
            po.wait_ge(sp_out, DEPTH * HEADS * 16 + 16)

        @block.scalar
        def _(ac):
            ac.sem_inc(acc_out, NT)
            ac.wait_ge(zeroed, 2)

            def hi(m0, p):
                ac.wait_ge(w_landed[p % 2], m0 * 16 + 32 * (p // 2 + 1))
                ac.wait_ge(w_used, m0 + p + 1)
                nc.scalar.activation(Whi[:, p % 2], raw[:, p % 2], ACT.Copy).then_inc(w_hi, 1)

            def t_hi_unit(s0, u, kind, i, col):
                bank = side[:, u % 2]
                ac.wait_ge(side_ready, s0 + u + 1)
                if kind == "p":
                    nc.scalar.activation(Ahi[:, i, 0:NPT * P], bank, ACT.Copy,
                                         scale=parl[:, col + i:col + i + 1]).then_inc(t_hi, 1)
                else:
                    for j in range(4):
                        k = 4 * i + j
                        last = nc.scalar.activation(Ahi[:, k, NPT * P:TOK], bank[:, j * P:(j + 1) * P], ACT.Copy,
                                                    scale=parl[:, col + k:col + k + 1])
                    last.then_inc(t_hi, 1)

            def t_hi_batch(s0, b, col):
                for n, (kind, i) in enumerate(T_BATCH[b]):
                    t_hi_unit(s0, T_FIRST[b] + n, kind, i, col)

            def squares(n, t):
                for j in range(2):
                    if t or j:
                        ac.wait_ge(sq_done, n * (2 * NT) + 2 * t + j)
                    nc.scalar.activation(stage[:].rearrange("p a b -> p (a b)"),
                                         H[:, t, j * (D // 2):(j + 1) * (D // 2)], ACT.Square,
                                         accum_out=ssq[:, t, j:j + 1]).then_inc(sq_done, 1)

            def stage_slot(n0, t):
                ac.wait_ge(stage_free, n0 + t + (2 if t == 0 else 1))
                return stage[:, t % 2]

            def wait_acc(q, t):
                if t < NT - 1:
                    ac.wait_ge(acc_ready, q * (NT - 1) + t + 1)
                else:
                    ac.wait_ge(w_used, q * PAIRS + PAIRS + 2)

            def to_z(q):
                for t in range(NT):
                    wait_acc(q, t)
                    nc.scalar.activation(Z[:, t], acc[:, t], ACT.Copy, scale=rstd[:, t:t + 1]).then_inc(acc_out, 1)

            def to_stage(q, n0, func, scaled):
                for t in range(NT):
                    slot = stage_slot(n0, t)
                    wait_acc(q, t)
                    nc.scalar.activation(slot, acc[:, t], func, scale=rstd[:, t:t + 1] if scaled else 1.0) \
                        .then_inc(acc_out, 1)

            with ac.Fori(0, DEPTH) as l:
                m0 = ac.snap(l * M_LAYER)
                s0 = ac.snap(l * S_LAYER)
                ac.wait_ge(parl_c, l + 1)
                hi(m0, 0)
                for b in range(PAIRS):
                    t_hi_batch(s0, b, PC_MIX)
                ac.wait_ge(stage_free, l * STAGES + 2)
                for t in range(NT):
                    squares(l * 2, t)
                with ac.Fori(0, HEADS) as h:
                    hh = ac.snap(l * HEADS + h)
                    m0 = ac.snap(l * M_LAYER + h * (G_HEAD * PAIRS))
                    q0 = ac.snap(l * G_LAYER + h * G_HEAD)
                    s0 = ac.snap(l * S_LAYER + h * H_UNITS + S_HEAD)
                    for p in range(PAIRS):
                        hi(m0, p + 1)
                    ac.wait_ge(rstd_done, l * 2 + 1)
                    ac.wait_ge(side_ready, s0)
                    to_z(q0)
                    for p in range(PAIRS):
                        hi(m0, PAIRS + p + 1)
                    ac.wait_ge(side_ready, s0 + U_KT)
                    ac.wait_ge(rot_done, hh * (2 * NT) + NT)
                    ac.wait_ge(upool_out, hh * (16 * (SB + 1)) + 16 * (SB + 1))
                    to_z(q0 + 1)

                    def decayed_chunk(c):
                        if c >= 2:
                            ac.wait_ge(side_ready, s0 + U_D[c - 2] + 1)
                        nc.scalar.activation(vd[:, c % 2], Z[:, c, DH:NW], ACT.Copy,
                                             scale=head[:, C_VP:C_VP + 1]).then_inc(vd_in, 1)

                    def decayed_stream(b):
                        if b >= 2:
                            ac.wait_ge(side_ready, s0 + U_DS[b - 2] + 1)
                        nc.scalar.activation(vdm[:, b % 2], Z[:, NPT, DH:NW], ACT.Copy,
                                             scale=head[:, C_VS + b:C_VS + b + 1]).then_inc(vdm_in, 1)

                    for p in range(PAIRS):
                        hi(m0, 2 * PAIRS + p + 1)
                        if p == 0:
                            ac.wait_ge(side_free, s0 + U_KT + 2)
                            for half in range(2):
                                diag = qTm[:, half].rearrange("p b n -> p (b n)")
                                for b in range(SB):
                                    last = nc.scalar.activation(
                                        diag[:, b * P + b * SL:b * P + (b + 1) * SL],
                                        qT[:, half, NPT * P + b * SL:NPT * P + (b + 1) * SL], ACT.Copy)
                            last.then_inc(qtm_in, 1)
                            ac.wait_ge(head_in, hh * 48 + 48)
                            ac.wait_ge(acc_out, q0 * NT + 3 * NT)
                            decayed_chunk(0)
                            decayed_chunk(1)
                            decayed_stream(0)
                            decayed_stream(1)
                        if p == 5:
                            decayed_chunk(2)
                            decayed_stream(2)
                            decayed_stream(3)
                        if p == 6:
                            decayed_chunk(3)
                            decayed_stream(4)
                            decayed_stream(5)
                        if p == 7:
                            decayed_stream(6)
                            decayed_stream(7)
                    to_stage(q0 + 2, ac.snap(l * STAGES + h * NT), ACT.Silu, True)

                m0 = ac.snap(l * M_LAYER + HEADS * G_HEAD * PAIRS)
                q0 = ac.snap(l * G_LAYER + HEADS * G_HEAD)
                s0 = ac.snap(l * S_LAYER + S_OUT)
                n0 = ac.snap(l * STAGES + HEADS * NT)
                t_hi_batch(s0, 0, PC_OUT)
                t_hi_batch(s0, 1, PC_OUT)
                for p in range(PAIRS):
                    hi(m0, p + 1)
                    if p + 2 < PAIRS:
                        t_hi_batch(s0, p + 2, PC_OUT)
                to_stage(q0, n0, ACT.Copy, False)
                with ac.Fori(1, G_OUT) as g:
                    mg = ac.snap(m0 + g * PAIRS)
                    for p in range(PAIRS):
                        hi(mg, p + 1)
                    to_stage(ac.snap(q0 + g), ac.snap(n0 + g * NT), ACT.Copy, False)

                m0 = ac.snap(l * M_LAYER + (HEADS * G_HEAD + G_OUT) * PAIRS)
                q0 = ac.snap(l * G_LAYER + HEADS * G_HEAD + G_OUT)
                s0 = ac.snap(l * S_LAYER + S_PG0)
                n0 = ac.snap(l * STAGES + (HEADS + G_OUT) * NT)
                t_hi_batch(s0, 0, PC_PLE)
                t_hi_batch(s0, 1, PC_PLE)
                for p in range(PAIRS):
                    hi(m0, p + 1)
                    if p + 2 < PAIRS:
                        t_hi_batch(s0, p + 2, PC_PLE)
                    if p == 1:
                        ac.wait_ge(stage_free, n0 + 2)
                    if 1 <= p <= NT:
                        squares(l * 2 + 1, p - 1)
                ac.wait_ge(rstd_done, l * 2 + 2)
                to_stage(q0, n0, ACT.Sigmoid, True)
                with ac.Fori(1, G_OUT - 1) as g:
                    mg = ac.snap(m0 + g * PAIRS)
                    for p in range(PAIRS):
                        hi(mg, p + 1)
                    to_stage(ac.snap(q0 + g), ac.snap(n0 + g * NT), ACT.Sigmoid, True)
                mg = ac.snap(m0 + (G_OUT - 1) * PAIRS)
                for p in range(PAIRS - 1):
                    hi(mg, p + 1)
                to_stage(q0 + (G_OUT - 1), n0 + (G_OUT - 1) * NT, ACT.Sigmoid, True)

            ac.wait_ge(stage_free, DEPTH * STAGES + 2)
            for t in range(NT):
                squares(2 * DEPTH, t)

        @block.vector
        def _(ve):
            ve.sem_inc(w_lo, 2)
            ve.sem_inc(side_free, 2)
            ve.sem_inc(os_free, 1)
            ve.sem_inc(stage_free, 2)

            class Chain:

                def __init__(self, s, base):
                    self.s, self.base, self.n = s, base, 0

                def __call__(self, ins):
                    ins.then_inc(self.s, 1)
                    self.n += 1

                def wait(self):
                    ve.wait_ge(self.s, self.base + self.n)

            def lo(m0, p):
                ve.wait_ge(w_hi, m0 + p + 1)
                nc.vector.tensor_tensor(Wlo[:, p % 2], raw[:, p % 2], Whi[:, p % 2].bitcast(F32), ALU.subtract) \
                    .then_inc(w_lo, 1)

            def t_lo_batch(s0, th0, b, col):
                for n, (kind, i) in enumerate(T_BATCH[b]):
                    u = T_FIRST[b] + n
                    ve.wait_ge(t_hi, th0 + u + 1)
                    if kind == "p":
                        last = nc.vector.scalar_tensor_tensor(
                            out=Alo[:, i, 0:NPT * P], in0=side[:, u % 2], scalar=parl[:, col + i:col + i + 1],
                            in1=Ahi[:, i, 0:NPT * P].bitcast(F32), op0=ALU.mult, op1=ALU.subtract)
                    else:
                        for j in range(4):
                            k = 4 * i + j
                            last = nc.vector.scalar_tensor_tensor(
                                out=Alo[:, k, NPT * P:TOK], in0=side[:, u % 2, j * P:(j + 1) * P],
                                scalar=parl[:, col + k:col + k + 1],
                                in1=Ahi[:, k, NPT * P:TOK].bitcast(F32), op0=ALU.mult, op1=ALU.subtract)
                    last.then_inc(side_free, 1)

            def mean_square(n):
                ve.wait_ge(sq_done, n * (2 * NT))
                ch = Chain(ch_ms, (n - 1) * 1)
                ch(nc.vector.tensor_tensor(ms[:], ssq[:, :, 0], ssq[:, :, 1], ALU.add))
                ch.wait()
                nc.vector.tensor_scalar(ms[:], ms[:], 1.0 / D, EPS, ALU.mult, ALU.add).then_inc(ms_done, 1)

            def rotate(ch, t, off, q):
                if ch.n:
                    ve.wait_ge(rot_done, ch.base + ch.n)
                ve.wait_ge(acc_out, q * NT + t + NT + 1)
                z = Z[:, t, off:off + DH].rearrange("p (a b) -> p a b", a=2)
                cos = rope[:, t, 0:P].unsqueeze(1).to_broadcast([P, 2, P])
                sin = rope[:, t, P:DH].unsqueeze(1).to_broadcast([P, 2, P])
                nc.vector.tensor_tensor(tA[:], z, cos, ALU.mult)
                ch(nc.vector.tensor_tensor(tB[:], z, sin, ALU.mult))
                ch.wait()
                nc.vector.tensor_tensor(z[:, 0], tA[:, 0], tB[:, 1], ALU.subtract)
                nc.vector.tensor_tensor(z[:, 1], tA[:, 1], tB[:, 0], ALU.add).then_inc(rot_done, 1)

            ve.wait_ge(par_t, 1)
            nc.vector.tensor_copy(par[:], side[:, 0, 0:DEPTH * PC_LAYER]).then_inc(par_c, 1)
            ve.wait_ge(par_c, 1)
            ve.wait_ge(const_in, 16 * (1 + 4 * DEPTH))
            for s in (*s_out, sp_out):
                ve.wait_ge(s, 16)

            with ve.Fori(0, DEPTH) as l:
                m0 = ve.snap(l * M_LAYER)
                s0 = ve.snap(l * S_LAYER)
                nc.vector.tensor_scalar(parl[:], par[:, one(l * PC_LAYER, PC_LAYER)], 1.0, None, ALU.mult) \
                    .then_inc(parl_c, 1)
                ve.wait_ge(parl_c, l + 1)
                lo(m0, 0)
                for b in range(PAIRS):
                    t_lo_batch(s0, l * (3 * T_UNITS), b, PC_MIX)
                mean_square(l * 2 + 1)
                with ve.Fori(0, HEADS) as h:
                    hh = ve.snap(l * HEADS + h)
                    m0 = ve.snap(l * M_LAYER + h * (G_HEAD * PAIRS))
                    s0 = ve.snap(l * S_LAYER + h * H_UNITS + S_HEAD)
                    z0 = ve.snap(hh * (2 * NT))
                    q0 = ve.snap(l * G_LAYER + h * G_HEAD)
                    rot = Chain(ch_rot, z0)
                    ret0 = HEADS * DH

                    def evac(u, write):
                        ve.wait_ge(side_ready, s0 + u + 1)
                        write(side[:, u % 2]).then_inc(side_free, 1)

                    def copy(dst):
                        return lambda bank: nc.vector.tensor_copy(
                            dst, bank[:, 0:dst.free_size()] if len(dst.shape) == 2 else
                            bank[:, 0:dst.free_size()].rearrange("p (a b) -> p a b", a=dst.shape[1]))

                    for p in range(PAIRS):
                        lo(m0, p + 1)

                    for p in range(PAIRS):
                        lo(m0, PAIRS + p + 1)
                        if p <= 2:
                            for t in ((0, 1), (2, 3), (4,))[p]:
                                rotate(rot, t, DH, q0)
                        if p == 1:
                            evac(U_BAND, copy(pooledT[:, 0, 0:NPT * P]))
                        if p == 2:
                            evac(U_BAND + 1, copy(pooledT[:, 1, 0:NPT * P]))
                        if p == 3:
                            evac(U_BAND + 2, copy(pooledT[:, :, NPT * P:TOK]))
                        if p == 4:
                            ve.wait_ge(hres_out, l * 16 + 16)
                            for i in range(2):
                                evac(U_MAP + i, lambda bank: nc.vector.tensor_scalar(
                                    H[:, 2 * i:2 * i + 2, one(h * DH, DH)],
                                    bank.rearrange("p (t c) -> p t c", t=2), 1.0, None, ALU.mult))
                        if p == 5:
                            evac(U_MAP + 2, lambda bank: nc.vector.tensor_scalar(
                                H[:, NPT, one(h * DH, DH)], bank[:, 0:DH], 1.0, None, ALU.mult))
                            evac(U_QT, copy(qT[:, 0, 0:NPT * P]))
                        if p == 6:
                            evac(U_QT + 1, copy(qT[:, 1, 0:NPT * P]))
                            evac(U_QT + 2, copy(qT[:, :, NPT * P:TOK]))

                    gn = Chain(ch_gn, hh * (2 * NT))

                    def normalize(t, bank):
                        gn(nc.vector.bn_stats(st6[:, t], bank[:, 0:DH]))
                        last = nc.vector.tensor_scalar(H[:, t, one(h * DH + ret0, DH)], bank[:, 0:DH], 1.0, None,
                                                       ALU.mult)
                        return last

                    def aggregate(t):
                        gn.wait()
                        settle(ve)
                        gn(nc.vector.bn_aggr(mv[:, t], st6[:, t]))

                    def output(c):
                        evac(U_O[c], lambda bank: normalize(c, bank))
                        aggregate(c)

                    def update(c):
                        if c == 0:
                            ve.wait_ge(sp_out, hh * 16 + 16)
                            evac(U_D[0], copy(Sp[:]))
                        else:
                            evac(U_D[c], lambda bank: nc.vector.scalar_tensor_tensor(
                                out=Sp[:].rearrange("p a b -> p (a b)"), in0=Sp[:].rearrange("p a b -> p (a b)"),
                                scalar=head[:, C_GP:C_GP + 1], in1=bank, op0=ALU.mult, op1=ALU.add))

                    def update_stream(b):
                        state = Ss[:, b % 4].rearrange("p a b -> p (a b)")
                        evac(U_DS[b], lambda bank: nc.vector.scalar_tensor_tensor(
                            out=state, in0=state, scalar=head[:, C_GS:C_GS + 1], in1=bank,
                            op0=ALU.mult, op1=ALU.add))

                    for p in range(PAIRS):
                        lo(m0, 2 * PAIRS + p + 1)
                        if p <= 2:
                            for t in ((0, 1), (2, 3), (4,))[p]:
                                rotate(rot, t, 0, q0 + 1)
                        if p == 2:
                            evac(U_KT, copy(kT[:, 0, 0:NPT * P]))
                            evac(U_KT + 1, copy(kT[:, 1, 0:NPT * P]))
                        if p == 3:
                            evac(U_KT + 2, copy(kT[:, :, NPT * P:TOK]))
                            evac(U_SC, lambda bank: nc.vector.tensor_tensor(
                                ST[:, 0:NPT], bank.rearrange("p (c n) -> p c n", c=NPT),
                                head[:, C_MASKP:C_MASKP + P].unsqueeze(1).to_broadcast([P, NPT, P]), ALU.mult))
                        if p == 4:
                            evac(U_SC + 1, lambda bank: nc.vector.tensor_tensor(
                                ST[:, NPT], bank[:, 0:P], head[:, C_MASKS:C_MASKS + P], ALU.mult))
                            output(0)
                            update(0)
                        if p == 5:
                            for b in range(4):
                                update_stream(b)
                            output(1)
                            update(1)
                        if p == 6:
                            output(2)
                            update(2)
                        if p == 7:
                            output(3)
                            update(3)
                            for b in range(4, 8):
                                update_stream(b)
                            ve.wait_ge(os_ready, hh + 1)
                            normalize(NPT, osb).then_inc(os_free, 1)
                            aggregate(NPT)
                    gate = Chain(ch_gate, hh * 3)
                    gn.wait()
                    gate(nc.vector.tensor_tensor(gv[:], mv[:, :, 1], head[:, C_D2:C_D2 + NT], ALU.mult))
                    gate.wait()
                    nc.vector.tensor_scalar(gv[:], gv[:], GN_EPS, None, ALU.add).then_inc(gn_in, 1)
                    ve.wait_ge(gn_pow, hh + 1)
                    gate(nc.vector.tensor_tensor(gr[:], gp[:], head[:, C_D:C_D + NT], ALU.mult))
                    gate.wait()
                    for t in range(NT):
                        o = H[:, t, one(h * DH + ret0, DH)]
                        last = nc.vector.tensor_scalar(o, o, mv[:, t, 0:1], gr[:, t:t + 1], ALU.subtract, ALU.mult)
                    gate(last)
                    gate.wait()
                    for t in range(NT):
                        both = H[:, t].rearrange("p (a b) -> p a b", a=2)[:, :, one(h * DH, DH)]
                        ve.wait_ge(acc_out, q0 * NT + 2 * NT + t + NT + 1)
                        last = nc.vector.tensor_tensor(both, both, stage[:, t % 2].rearrange("p (a b) -> p a b", a=2),
                                                       ALU.mult).then_inc(stage_free, 1)
                    assert gn.n == 2 * NT and rot.n == 2 * NT and gate.n == 3

                m0 = ve.snap(l * M_LAYER + HEADS * G_HEAD * PAIRS)
                s0 = ve.snap(l * S_LAYER + S_OUT)
                th0 = ve.snap(l * (3 * T_UNITS) + T_UNITS)
                q0 = ve.snap(l * G_LAYER + HEADS * G_HEAD)

                def add_residual(g, q):
                    ve.wait_ge(res_in, l * (G_OUT * 16) + g * 16 + 16)
                    for t in range(NT):
                        ve.wait_ge(acc_out, q * NT + t + NT + 1)
                        nc.vector.tensor_tensor(H[:, t, one(g * NW, NW)], stage[:, t % 2], Z[:, t], ALU.add) \
                            .then_inc(stage_free, 1)

                t_lo_batch(s0, th0, 0, PC_OUT)
                t_lo_batch(s0, th0, 1, PC_OUT)
                for p in range(PAIRS):
                    lo(m0, p + 1)
                    if p + 2 < PAIRS:
                        t_lo_batch(s0, th0, p + 2, PC_OUT)
                    for i in ((), (0, 1), (2, 3))[max(p - 5, 0)]:
                        u = T_UNITS + i
                        ve.wait_ge(side_ready, s0 + u + 1)
                        dst = pT[:, i, 0:NPT * P] if i < 2 else pT[:, i - 2, NPT * P:TOK]
                        nc.vector.tensor_copy(dst, side[:, u % 2, 0:dst.free_size()]).then_inc(side_free, 1)
                add_residual(0, q0)
                with ve.Fori(1, G_OUT) as g:
                    mg = ve.snap(m0 + g * PAIRS)
                    for p in range(PAIRS):
                        lo(mg, p + 1)
                    add_residual(g, ve.snap(q0 + g))

                m0 = ve.snap(l * M_LAYER + (HEADS * G_HEAD + G_OUT) * PAIRS)
                s0 = ve.snap(l * S_LAYER + S_PG0)
                q0 = ve.snap(l * G_LAYER + HEADS * G_HEAD + G_OUT)
                th0 = ve.snap(l * (3 * T_UNITS) + 2 * T_UNITS)

                def ple(s1, u0, i):
                    ve.wait_ge(side_ready, s1 + u0 + i + 1)
                    dst = Z[:, i] if i < NPT else Z[:, NPT, (i - NPT) * DH:(i - NPT + 1) * DH]
                    nc.vector.tensor_copy(dst, side[:, (u0 + i) % 2, 0:dst.free_size()]).then_inc(side_free, 1)

                def add_gated(g, q):
                    ch = Chain(ch_pg, l * (G_OUT * NT) + g * NT)
                    for t in range(NT):
                        ve.wait_ge(acc_out, q * NT + t + NT + 1)
                        ch(nc.vector.tensor_tensor(stage[:, t % 2], stage[:, t % 2], Z[:, t], ALU.mult))
                        ch.wait()
                        nc.vector.tensor_tensor(H[:, t, one(g * NW, NW)], H[:, t, one(g * NW, NW)], stage[:, t % 2],
                                                ALU.add).then_inc(stage_free, 1)

                t_lo_batch(s0, th0, 0, PC_PLE)
                t_lo_batch(s0, th0, 1, PC_PLE)
                for p in range(PAIRS):
                    lo(m0, p + 1)
                    if p + 2 < PAIRS:
                        t_lo_batch(s0, th0, p + 2, PC_PLE)
                    for i in ((), (0,), (1, 2, 3), (4, 5))[max(p - 4, 0)]:
                        ple(s0, T_UNITS, i)
                mean_square(l * 2 + 2)
                ve.wait_ge(side_free, s0 + T_UNITS + PLE_UNITS + 2)
                add_gated(0, q0)
                with ve.Fori(1, G_OUT - 1) as g:
                    mg = ve.snap(m0 + g * PAIRS)
                    s1 = ve.snap(l * S_LAYER + g * PLE_UNITS + (S_PG - PLE_UNITS))
                    for p in range(PAIRS):
                        lo(mg, p + 1)
                        if 1 <= p <= PLE_UNITS:
                            ple(s1, 0, p - 1)
                    ve.wait_ge(side_free, s1 + PLE_UNITS + 2)
                    add_gated(g, ve.snap(q0 + g))
                mg = ve.snap(m0 + (G_OUT - 1) * PAIRS)
                s1 = ve.snap(l * S_LAYER + S_LAYER - PLE_UNITS)
                for p in range(PAIRS):
                    if p < PAIRS - 1:
                        lo(mg, p + 1)
                    if 1 <= p <= PLE_UNITS:
                        ple(s1, 0, p - 1)
                ve.wait_ge(side_free, s1 + PLE_UNITS + 2)
                add_gated(G_OUT - 1, q0 + (G_OUT - 1))

            mean_square(2 * DEPTH + 1)
            ve.wait_ge(rstd_done, 2 * DEPTH + 1)
            ve.wait_ge(gfin_in, 16)
            for t in range(NT):
                nc.vector.scalar_tensor_tensor(out=H[:, t], in0=H[:, t], scalar=rstd[:, t:t + 1], in1=gfin,
                                               op0=ALU.mult, op1=ALU.mult).then_inc(y_in, 1)

        @block.tensor
        def _(pe):
            pe.sem_inc(w_used, 2)
            pe.wait_ge(const_in, 16 * (1 + 4 * DEPTH))
            n = DEPTH * PC_LAYER
            nc.tensor.transpose(side[:, 0, 0:n], pstage, ident[0:n, 0:n]).then_inc(par_t, 1)
            pe.wait_ge(par_c, 1)

            def pair(m0, p, a0):
                pe.wait_ge(w_lo, m0 + p + 3)
                for kk in range(2):
                    k = 2 * p + kk
                    for t in range(NT):
                        if k == 0:
                            pe.wait_ge(acc_out, a0 + t + 1)
                        tok = slice(t * P, (t + 1) * P)
                        nc.tensor.matmul(acc[:, t], Ahi[:, k, tok], Whi[:, p % 2, kk], start=(k == 0), stop=False)
                        nc.tensor.matmul(acc[:, t], Ahi[:, k, tok], Wlo[:, p % 2, kk], start=False, stop=False)
                        mm = nc.tensor.matmul(acc[:, t], Alo[:, k, tok], Whi[:, p % 2, kk], start=False,
                                              stop=(k == KT - 1))
                        if kk == 1 and t == NT - 1:
                            mm.then_inc(w_used, 1)
                        elif k == KT - 1:
                            mm.then_inc(acc_ready, 1)

            def open_unit(s0, u):
                pe.wait_ge(side_free, s0 + u + 1)
                return side[:, u % 2]

            def t_batch(s0, b):
                for n, (kind, i) in enumerate(T_BATCH[b]):
                    bank = open_unit(s0, T_FIRST[b] + n)
                    for j in range(4):
                        t, k = (j, i) if kind == "p" else (NPT, 4 * i + j)
                        last = nc.tensor.transpose(bank[:, j * P:(j + 1) * P], H[:, t, k * P:(k + 1) * P], ident[:])
                    last.then_inc(side_ready, 1)

            def t_done(s0, b):
                pe.wait_ge(side_free, s0 + T_FIRST[b + 1] + 2)

            def mm(out, lhsT, rhs, start=True, stop=True):
                return nc.tensor.matmul(out, lhsT, rhs, start=start, stop=stop)

            with pe.Fori(0, DEPTH) as l:
                s0 = pe.snap(l * S_LAYER)
                pe.wait_ge(h_in, 32)
                pe.wait_ge(stage_free, l * STAGES + 2)
                for b in range(PAIRS):
                    t_batch(s0, b)
                t_done(s0, PAIRS - 1)
                settle(pe)
                with pe.Fori(0, HEADS) as h:
                    hh = pe.snap(l * HEADS + h)
                    m0 = pe.snap(l * M_LAYER + h * (G_HEAD * PAIRS))
                    a0 = pe.snap(l * (G_LAYER * NT) + h * (G_HEAD * NT))
                    s0 = pe.snap(l * S_LAYER + h * H_UNITS + S_HEAD)
                    z0 = pe.snap(hh * (2 * NT))

                    for p in range(PAIRS):
                        pair(m0, p, a0)

                    def band(c):
                        bank = open_unit(s0, U_BAND + c)
                        for j in range(NPT if c < 2 else 2):
                            t, ch = (j, c) if c < 2 else (NPT, j)
                            out = bank[:, j * P:(j + 1) * P]
                            cols = slice(ch * P, (ch + 1) * P)
                            if t == 0:
                                last = mm(out, Z[:, 0, cols], head[:, C_BAND0:C_BAND0 + P])
                            elif t < NPT:
                                mm(out, Z[:, t, cols], head[:, C_BAND:C_BAND + P], stop=False)
                                last = mm(out, Z[:, t - 1, cols], head[:, C_PREV:C_PREV + P], start=False)
                            else:
                                r = SB * HIST
                                mm(out, Z[:, t, cols], head[:, C_BANDS:C_BANDS + P], stop=False)
                                last = mm(out, hist[0:r, cols], head[0:r, C_HISTS:C_HISTS + P], start=False)
                        last.then_inc(side_ready, 1)

                    def pool_map(i):
                        bank = open_unit(s0, U_MAP + i)
                        for j, t in enumerate(((0, 1), (2, 3), (4,))[i]):
                            for c in range(2):
                                last = mm(bank[:, j * DH:(j + 1) * DH], pooledT[:, c, t * P:(t + 1) * P],
                                          wpool[:, c], start=(c == 0), stop=(c == 1))
                        last.then_inc(side_ready, 1)

                    def turn(u, i, off):
                        bank = open_unit(s0, u + i)
                        for j in range(NPT if i < 2 else 2):
                            t, half = (j, i) if i < 2 else (NPT, j)
                            last = nc.tensor.transpose(bank[:, j * P:(j + 1) * P],
                                                       Z[:, t, off + half * P:off + (half + 1) * P], ident[:])
                        last.then_inc(side_ready, 1)

                    for p in range(PAIRS):
                        pair(m0 + PAIRS, p, a0 + NT)
                        if p == 1:
                            pe.wait_ge(acc_out, a0 + 2 * NT)
                            pe.wait_ge(head_in, hh * 48 + 48)
                            band(0)
                        if p == 2:
                            band(1)
                        if p == 3:
                            band(2)
                        if p == 4:
                            pe.wait_ge(side_free, s0 + U_MAP + 2)
                            pool_map(0)
                            pool_map(1)
                        if p == 5:
                            pool_map(2)
                            pe.wait_ge(rot_done, z0 + NT)
                            turn(U_QT, 0, DH)
                        if p == 6:
                            turn(U_QT, 1, DH)
                            turn(U_QT, 2, DH)

                    def scores(u, tiles):
                        bank = open_unit(s0, u)
                        for j, t in enumerate(tiles):
                            for half in range(2):
                                last = mm(bank[:, j * P:(j + 1) * P], kT[:, half, t * P:(t + 1) * P],
                                          qT[:, half, t * P:(t + 1) * P], start=(half == 0), stop=(half == 1))
                        last.then_inc(side_ready, 1)

                    def output(c):
                        bank = open_unit(s0, U_O[c])
                        last = mm(bank[:, 0:DH], ST[:, c], Z[:, c, DH:NW], stop=(c == 0))
                        if c:
                            pe.wait_ge(side_free, s0 + U_D[c - 1] + 3)
                            for half in range(2):
                                last = mm(bank[:, 0:DH], qT[:, half, c * P:(c + 1) * P], Sp[:, half], start=False,
                                          stop=(half == 1))
                        last.then_inc(side_ready, 1)

                    def update(c):
                        bank = open_unit(s0, U_D[c])
                        pe.wait_ge(vd_in, hh * NPT + c + 1)
                        for half in range(2):
                            last = mm(bank[:, half * DH:(half + 1) * DH], Z[:, c, half * P:(half + 1) * P],
                                      vd[:, c % 2])
                        last.then_inc(side_ready, 1)

                    def stream_output(b):
                        pe.wait_ge(s_in[b % 4], hh * 32 + 16 * (b // 4 + 1))
                        for half in range(2):
                            last = mm(osb[:, 0:DH], qTm[:, half, b], Ss[:, b % 4, half], start=False,
                                      stop=(b == SB - 1 and half == 1))
                        if b == SB - 1:
                            last.then_inc(os_ready, 1)

                    def stream_update(b):
                        bank = open_unit(s0, U_DS[b])
                        pe.wait_ge(vdm_in, hh * SB + b + 1)
                        for half in range(2):
                            last = mm(bank[:, half * DH:(half + 1) * DH], Z[:, NPT, half * P:(half + 1) * P],
                                      vdm[:, b % 2])
                        last.then_inc(side_ready, 1)

                    for p in range(PAIRS):
                        pair(m0 + 2 * PAIRS, p, a0 + 2 * NT)
                        if p == 2:
                            pe.wait_ge(rot_done, z0 + 2 * NT)
                            turn(U_KT, 0, 0)
                            turn(U_KT, 1, 0)
                        if p == 3:
                            turn(U_KT, 2, 0)
                            pe.wait_ge(side_free, s0 + U_KT + 4)
                            scores(U_SC, range(NPT))
                        if p == 4:
                            pe.wait_ge(side_free, s0 + U_KT + 5)
                            scores(U_SC + 1, (NPT,))
                            pe.wait_ge(side_free, s0 + U_SC + 3)
                            output(0)
                            update(0)
                        if p == 5:
                            pe.wait_ge(side_free, s0 + U_SC + 4)
                            pe.wait_ge(qtm_in, hh + 1)
                            pe.wait_ge(os_free, hh + 1)
                            mm(osb[:, 0:DH], ST[:, NPT], Z[:, NPT, DH:NW], stop=False)
                            for b in range(4):
                                stream_output(b)
                            for b in range(4):
                                stream_update(b)
                            output(1)
                            update(1)
                        if p == 6:
                            output(2)
                            update(2)
                        if p == 7:
                            for b in range(4, 8):
                                stream_output(b)
                            output(3)
                            update(3)
                            for b in range(4, 8):
                                stream_update(b)

                m0 = pe.snap(l * M_LAYER + HEADS * G_HEAD * PAIRS)
                a0 = pe.snap(l * (G_LAYER * NT) + HEADS * G_HEAD * NT)
                s0 = pe.snap(l * S_LAYER + S_OUT)
                pe.wait_ge(stage_free, l * STAGES + (HEADS * NT + 2))
                t_batch(s0, 0)
                t_batch(s0, 1)
                for p in range(PAIRS):
                    t_done(s0, p)
                    pair(m0, p, a0)
                    if p + 2 < PAIRS:
                        t_batch(s0, p + 2)
                    if p == 6:
                        pe.wait_ge(p_in, l * 32 + 32)
                    for i in ((), (0, 1), (2, 3))[max(p - 5, 0)]:
                        bank = open_unit(s0, T_UNITS + i)
                        for j in range(NPT if i < 2 else 1):
                            t, half = (j, i) if i < 2 else (NPT, i - 2)
                            last = nc.tensor.transpose(bank[:, j * P:(j + 1) * P],
                                                       P5[:, t, half * P:(half + 1) * P], ident[:])
                        last.then_inc(side_ready, 1)
                with pe.Fori(1, G_OUT) as g:
                    mg, ag = pe.snap(m0 + g * PAIRS), pe.snap(a0 + g * NT)
                    for p in range(PAIRS):
                        pair(mg, p, ag)

                m0 = pe.snap(l * M_LAYER + (HEADS * G_HEAD + G_OUT) * PAIRS)
                a0 = pe.snap(l * (G_LAYER * NT) + (HEADS * G_HEAD + G_OUT) * NT)
                s0 = pe.snap(l * S_LAYER + S_PG0)

                def ple(s1, u0, i):
                    bank = open_unit(s1, u0 + i)
                    t = min(i, NPT)
                    cols = slice(0, NW) if i < NPT else slice((i - NPT) * DH, (i - NPT + 1) * DH)
                    out = bank[:, 0:NW if i < NPT else DH]
                    for c in range(2):
                        last = mm(out, pT[:, c, t * P:(t + 1) * P], wple[:, c, cols], start=(c == 0), stop=(c == 1))
                    last.then_inc(side_ready, 1)

                pe.wait_ge(stage_free, l * STAGES + ((HEADS + G_OUT) * NT + 2))
                t_batch(s0, 0)
                t_batch(s0, 1)
                for p in range(PAIRS):
                    t_done(s0, p)
                    pair(m0, p, a0)
                    if p + 2 < PAIRS:
                        t_batch(s0, p + 2)
                    if p == 5:
                        pe.wait_ge(wple_in, l * (16 * G_OUT) + 16)
                    for i in ((), (0,), (1, 2, 3), (4, 5))[max(p - 4, 0)]:
                        ple(s0, T_UNITS, i)
                with pe.Fori(1, G_OUT) as g:
                    mg, ag = pe.snap(m0 + g * PAIRS), pe.snap(a0 + g * NT)
                    s1 = pe.snap(l * S_LAYER + g * PLE_UNITS + (S_PG - PLE_UNITS))
                    for p in range(PAIRS):
                        pair(mg, p, ag)
                        if p == 1:
                            pe.wait_ge(wple_in, l * (16 * G_OUT) + g * 16 + 16)
                        if 1 <= p <= PLE_UNITS:
                            ple(s1, 0, p - 1)


_INS = ["x_prompt", "x_sample", "p_prompt", "p_sample", "state_pool", "state_ret", "g_mix", "w_in", "w_pool",
        "pool_scale", "g_gn", "w_out", "g_ple", "w_pg", "w_ple", "g_final"]
_OUTS = [("y_prompt", (1, 512, D)), ("y_sample", (SB, SL, D)),
         ("new_pool_prompt", (DEPTH, 1, HIST, HEADS * DH)), ("new_ret_prompt", (DEPTH, 1, HEADS, DH, DH)),
         ("new_pool_sample", (DEPTH, SB, HIST, HEADS * DH)), ("new_ret_sample", (DEPTH, SB, HEADS, DH, DH))]


def _tables():
    import numpy as np
    n = np.arange(P)
    pos = np.concatenate([np.arange(NPT * P), PAST + np.arange(P) % SL]).astype(np.float32)
    half = DH // 2
    inv = np.float32(1.0) / (np.float32(10000.0) ** (np.arange(half, dtype=np.float32) / np.float32(half)))
    ang = (pos[:, None] * inv[None, :].astype(np.float32)).astype(np.float32).astype(np.float64)
    rope = np.concatenate([np.cos(ang), np.sin(ang)], axis=1).reshape(NT, P, DH).transpose(1, 0, 2)

    head = np.zeros((HEADS, P, C_HEAD))
    b, i = n // SL, n % SL
    same = b[:, None] == b[None, :]
    key_scale = DH ** -0.5
    for h in range(HEADS):
        g = 1.0 - 2.0 ** (-5.0 - h)
        t = head[h]
        t[:, C_MASKP:C_MASKP + P] = (n[:, None] <= n[None, :]) * g ** -(n[:, None] + 1.0) * key_scale
        t[:, C_MASKS:C_MASKS + P] = (same & (i[:, None] <= i[None, :])) * g ** -(i[:, None] + 1.0) * key_scale
        t[:, C_D:C_D + NPT] = (g ** (n + 1.0))[:, None]
        t[:, C_D + NPT] = g ** (i + 1.0)
        t[:, C_D2:C_D2 + NT] = t[:, C_D:C_D + NT] ** 2
        t[:, C_VP] = g ** (P - 1.0 - n) * key_scale
        t[:, C_GP], t[:, C_GS] = g ** P, g ** SL
        t[:, C_VS:C_VS + SB] = (b[:, None] == np.arange(SB)) * (g ** (SL - 1.0 - i) * key_scale)[:, None]
        w = WINDOWS[h]
        inside = (n[:, None] <= n[None, :]) & (n[:, None] > n[None, :] - w)
        eye = np.eye(P)
        t[:, C_BAND0:C_BAND0 + P] = inside / np.minimum(w, n + 1.0)[None, :] - eye
        t[:, C_BAND:C_BAND + P] = inside / w - eye
        t[:, C_PREV:C_PREV + P] = (n[:, None] - P > n[None, :] - w) / w
        t[:, C_BANDS:C_BANDS + P] = (same & inside) / w - eye
        r = np.arange(SB * HIST)
        t[0:SB * HIST, C_HISTS:C_HISTS + P] = ((r // HIST)[:, None] == b[None, :]) & \
            ((r % HIST - HIST)[:, None] > i[None, :] - w)
        t[0:SB * HIST, C_HISTS:C_HISTS + P] /= w
    return {"c_ident": np.eye(P, dtype=np.float32), "c_rope": rope.astype(np.float32),
            "c_head": head.astype(np.float32)}


def kernel(**inputs):
    import numpy as _np
    import concourse.bacc as _bacc
    from concourse import mybir as _mybir
    from concourse.bass_utils import run_bass_kernel_spmd as _run

    nc = _bacc.Bacc("TRN2", target_bir_lowering=False, num_devices=1)
    arrays, a = {}, {}
    for name, value in [(n, inputs[n]) for n in _INS] + list(_tables().items()):
        value = _np.ascontiguousarray(value)
        arrays[f"in_{name}"] = value
        a[name] = nc.dram_tensor(f"in_{name}", value.shape, _mybir.dt.from_np(value.dtype), kind="ExternalInput").ap()
    for name, shape in _OUTS:
        a[name] = nc.dram_tensor(f"out_{name}", shape, F32, kind="ExternalOutput").ap()
    build(nc, a)
    r = _run(nc, [arrays], core_ids=[0])
    return tuple(r.results[0][f"out_{name}"] for name, _ in _OUTS)
```

```python
from contextlib import ExitStack

import concourse.bass as bass
from concourse import mybir

F32 = mybir.dt.float32
F32R = mybir.dt.float32r
ALU = mybir.AluOpType
ACT = mybir.ActivationFunctionType

P = 128
D = 2048
DEPTH = 2
NT = 5
TOK = NT * P
NPT = 4
SB, SL = 8, 16
HEADS = 4
DH = 256
HIST = 15
WINDOWS = (2, 4, 8, 16)
PAST = 128
PLE = 256
NW = 512
KT = D // P
PAIRS = KT // 2
EPS, GN_EPS = 1e-6, 1e-5

G_HEAD = 3
G_OUT = D // NW
G_LAYER = HEADS * G_HEAD + 2 * G_OUT
M_LAYER = G_LAYER * PAIRS

T_UNITS = 20
H_UNITS = 30
PT_UNITS = 4
PLE_UNITS = 6
S_PRO = 0
S_HEAD = S_PRO + T_UNITS
S_OUT = S_HEAD + HEADS * H_UNITS
S_PG0 = S_OUT + T_UNITS + PT_UNITS
S_PG = S_PG0 + T_UNITS + PLE_UNITS
S_LAYER = S_PG + (G_OUT - 1) * PLE_UNITS
U_BAND, U_MAP, U_QT, U_KT, U_SC = 0, 3, 6, 9, 12
U_O = (14, 20, 22, 24)
U_D = (15, 21, 23, 25)
H_ADDS = G_OUT - 1 + NT
U_DS = (16, 17, 18, 19, 26, 27, 28, 29)
STAGES = NT * (HEADS + 2 * G_OUT)

C_MASKP, C_MASKS, C_BAND0, C_BAND, C_PREV, C_BANDS, C_HISTS = (i * P for i in range(7))
C_D = 7 * P
C_D2 = C_D + NT
C_VP = C_D2 + NT
C_GP, C_GS = C_VP + 1, C_VP + 2
C_VS = C_GS + 1
C_HEAD = C_VS + SB + 3

PC_MIX, PC_OUT, PC_PLE, PC_LAYER = 0, KT, 2 * KT, 3 * KT

K_PLAIN = tuple(range(KT))
K_OUT = (0, 1, 2, 3, 4, 5, 8, 9, 10, 11, 12, 13, 6, 7, 14, 15)
T_ORDER = {ks: [u for i in range(KT) for u in [(ks[i],)] + ([ks[i:i + 4]] if i % 4 == 0 else [])]
           for ks in (K_PLAIN, K_OUT)}
T_PROMPT = tuple(i + (i + 3) // 4 for i in range(KT))
T_SAMPLE = {i: i + i // 4 + 1 for i in range(0, KT, 4)}
T_FIRST = 3


def t_slot(s):
    return range(min(T_FIRST + 2 * s, T_UNITS), min(T_FIRST + 2 * s + 2, T_UNITS))


def build(nc, a):
    with ExitStack() as ctx:
        def sb(name, shape, dt=F32):
            return ctx.enter_context(nc.sbuf_tensor(name, shape, dt))

        def psum(name, shape):
            return ctx.enter_context(nc.psum_tensor(name, shape, F32))

        def sem(name):
            return ctx.enter_context(nc.semaphore(name))

        H = sb("H", [P, NT, D])
        Ahi = sb("Ahi", [P, KT, TOK], F32R)
        Alo = sb("Alo", [P, KT, TOK], F32R)
        raw = sb("raw", [P, 2, 2, NW])
        Whi = sb("Whi", [P, 2, 2, NW], F32R)
        Wlo = sb("Wlo", [P, 2, 2, NW], F32R)
        Z = sb("Z", [P, NT, NW])
        qT = sb("qT", [P, 2, TOK])
        kT = sb("kT", [P, 2, TOK])
        ST = sb("ST", [P, NT, P])
        Sp = sb("Sp", [P, 2, DH])
        vd = sb("vd", [P, 2, DH])
        vdm = sb("vdm", [P, 2, DH])
        qTm = sb("qTm", [P, 2, SB, P])
        Ss = sb("Ss", [P, 4, 2, DH])
        head = sb("head", [P, C_HEAD])
        wpool = sb("wpool", [P, 2, DH])
        hist = sb("hist", [P, DH])
        rope = sb("rope", [P, NT, DH])
        stage = sb("stage", [P, 2, NW])
        tA = sb("tA", [P, 2, P])
        tB = sb("tB", [P, 2, P])
        ident = sb("ident", [P, P])
        par = sb("par", [P, DEPTH * PC_LAYER])
        parl = sb("parl", [P, PC_LAYER])
        ssq = sb("ssq", [P, NT, 2])
        ms = sb("ms", [P, NT])
        rstd = sb("rstd", [P, NT])
        mhalf = sb("mhalf", [P, NT])
        st6 = sb("st6", [P, NT, 6])
        mv = sb("mv", [P, NT, 2])
        gv = sb("gv", [P, NT])
        gp = sb("gp", [P, NT])
        gr = sb("gr", [P, NT])

        pooledT, P5, pT = kT, kT[:].rearrange("p a b -> p (a b)").rearrange("p (t c) -> p t c", t=NT), qT
        wple = Ss[:, 0:2].rearrange("p a b c -> p (a b c)").rearrange("p (k n) -> p k n", k=2)
        gfin = Z[:].rearrange("p t n -> p (t n)")[:, 0:D]
        pstage = stage[0:DEPTH * PC_LAYER, 0, 0:P]

        acc = psum("acc", [P, NT, NW])
        side = psum("side", [P, 2, NW])
        osb = psum("osb", [P, NW])

        hres = nc.dram_tensor("h_residual", [TOK, D], F32, kind="Internal").ap()

        settled = sem("settled")
        const_in = sem("const_in")
        par_t, par_c, parl_c, zeroed = sem("par_t"), sem("par_c"), sem("parl_c"), sem("zeroed")
        x_in = [sem(f"x_in{c}") for c in range(4)]
        h_upd = sem("h_upd")
        w_landed = [sem("w_landed0"), sem("w_landed1")]
        w_hi, w_lo, w_used = sem("w_hi"), sem("w_lo"), sem("w_used")
        acc_ready = sem("acc_ready")
        acc_out = sem("acc_out")
        side_ready, side_free = sem("side_ready"), sem("side_free")
        t_high = sem("t_high")
        sq_done, ms_done, rstd_done, rstd_ok = sem("sq_done"), sem("ms_done"), sem("rstd_done"), sem("rstd_ok")
        rot_done = sem("rot_done")
        head_in = sem("head_in")
        upool_out = sem("upool_out")
        s_in = [sem(f"s_in{j}") for j in range(4)]
        s_out = [sem(f"s_out{j}") for j in range(4)]
        sp_out = sem("sp_out")
        qtm_in, vd_in, vdm_in = sem("qtm_in"), sem("vd_in"), sem("vdm_in")
        os_ready, os_free = sem("os_ready"), sem("os_free")
        gn_in, gn_pow = sem("gn_in"), sem("gn_pow")
        stage_free = sem("stage_free")
        hres_out, res_in = sem("hres_out"), sem("res_in")
        p_in, wple_in = sem("p_in"), sem("wple_in")
        ch_rot, ch_gn, ch_gate, ch_ms, ch_pg, ch_fin = (sem(n) for n in
            ("ch_rot", "ch_gn", "ch_gate", "ch_ms", "ch_pg", "ch_fin"))
        gfin_in, y_in, y_out = sem("gfin_in"), sem("y_in"), sem("y_out")

        w_in_v = a["w_in"].rearrange("l (k p) (s c) -> l p k s c", p=P, s=6)
        w_out_v = a["w_out"].rearrange("l (k p) c -> l p k c", p=P)
        w_pg_v = a["w_pg"].rearrange("l (k p) c -> l p k c", p=P)
        w_ple_v = a["w_ple"].rearrange("l (k p) c -> l p k c", p=P)
        w_pool_v = a["w_pool"].rearrange("l g (k p) c -> l g p k c", p=P)
        st_v = a["state_ret"].rearrange("l b h (k p) c -> l b h p k c", p=P)
        nst_v = a["new_ret_sample"].rearrange("l b h (k p) c -> l b h p k c", p=P)
        nsp_v = a["new_ret_prompt"].rearrange("l b h (k p) c -> l b h p k c", p=P)
        hist_v = a["state_pool"].rearrange("l b j c -> l (b j) c")
        hres_v = hres.rearrange("(t p) n -> p t n", p=P)
        one = bass.ds

        block = ctx.enter_context(nc.Block())

        def settle(e):
            e.sem_inc(settled, 1)

        def load_x(e, c):
            cols = slice(c * NW, (c + 1) * NW)
            e.dma_start(H[:, 0:NPT, cols], a["x_prompt"][:, :, cols].rearrange("b (t p) n -> p (b t) n", p=P)) \
                .then_inc(x_in[c], 16)
            e.dma_start(H[:, NPT, cols], a["x_sample"][:, :, cols].rearrange("b s n -> (b s) n")) \
                .then_inc(x_in[c], 16)

        @block.sync
        def _(sp):
            load_x(sp, 0)

            with sp.Fori(0, DEPTH) as l:
                with sp.Fori(0, HEADS) as h:
                    for j, segs in enumerate((slice(0, 3, 2), slice(3, 5), slice(1, 6, 4))):
                        m0 = sp.snap(l * M_LAYER + h * (G_HEAD * PAIRS) + j * PAIRS)
                        for p in range(PAIRS):
                            src = w_in_v[one(l, 1), :, 2 * p:2 * p + 2, segs, one(h * DH, DH)]
                            sp.wait_ge(w_lo, m0 + p + 1)
                            for kk in range(2):
                                sp.dma_start(raw[:, p % 2, kk, :].rearrange("p (s c) -> p s c", s=2),
                                             src[:, :, kk].rearrange("l p s c -> p (l s) c")) \
                                    .then_inc(w_landed[p % 2], 16)
                for base, view, ks in ((HEADS * G_HEAD, w_out_v, K_OUT), (HEADS * G_HEAD + G_OUT, w_pg_v, K_PLAIN)):
                    with sp.Fori(0, G_OUT) as g:
                        m0 = sp.snap(l * M_LAYER + g * PAIRS + base * PAIRS)
                        for p in range(PAIRS):
                            src = view[one(l, 1), :, ks[2 * p]:ks[2 * p] + 2, one(g * NW, NW)]
                            sp.wait_ge(w_lo, m0 + p + 1)
                            for kk in range(2):
                                sp.dma_start(raw[:, p % 2, kk, :], src[:, :, kk].rearrange("l p c -> p (l c)")) \
                                    .then_inc(w_landed[p % 2], 16)

            for t in range(NT):
                sp.wait_ge(y_in, t + 1)
                dst = a["y_prompt"][0, t * P:(t + 1) * P, :] if t < NPT else \
                    a["y_sample"].rearrange("b s n -> (b s) n")
                sp.dma_start(dst, H[:, t, :]).then_inc(y_out, 16)
            sp.wait_ge(y_out, 16 * NT)

        @block.gpsimd
        def _(po):
            po.dma_start(ident[:], a["c_ident"]).then_inc(const_in, 16)
            for c in range(1, 4):
                load_x(po, c)
            for l in range(DEPTH):
                r = l * PC_LAYER
                for src, r0, n in ((a["g_mix"], 0, 16), (a["pool_scale"], 16, 8), (a["g_gn"], 24, 8),
                                   (a["g_ple"], 32, 16)):
                    po.dma_start(stage[r + r0:r + r0 + n, 0, 0:P],
                                 src[l, :].rearrange("(k c) -> k c", c=P)).then_inc(const_in, 16)
            for t in range(NT):
                po.dma_start(rope[:, t], a["c_rope"][:, t]).then_inc(s_out[t] if t < 4 else sp_out, 16)
            po.memset(qTm[:], 0.0).then_inc(zeroed, 1)
            po.memset(mhalf[:], -0.5).then_inc(zeroed, 1)
            po.wait_ge(zeroed, 2)

            def rsqrt(n):
                po.wait_ge(ms_done, n)
                settle(po)
                nc.gpsimd.tensor_tensor(rstd[:], ms[:], mhalf[:], ALU.pow).then_inc(rstd_done, 1)

            with po.Fori(0, DEPTH) as l:
                for c in range(4):
                    po.wait_ge(x_in[c], 32)
                po.wait_ge(h_upd, l * H_ADDS + 1)
                settle(po)
                po.dma_start(hres_v, H[:]).then_inc(hres_out, 16)
                rsqrt(l * 2 + 1)
                settle(po)
                with po.Fori(0, HEADS) as h:
                    hh = po.snap(l * HEADS + h)
                    s0 = po.snap(l * S_LAYER + h * H_UNITS + S_HEAD)
                    po.wait_ge(stage_free, l * STAGES + h * NT + 2)
                    settle(po)
                    po.dma_start(head[:], a["c_head"][one(h, 1)].rearrange("o p c -> p (o c)")).then_inc(head_in, 16)
                    po.dma_start(wpool[:], w_pool_v[one(l, 1), one(h, 1)].rearrange("l g p k c -> p (l g k) c")) \
                        .then_inc(head_in, 16)
                    po.dma_start(hist[0:SB * HIST, :], hist_v[one(l, 1), :, one(h * DH, DH)]
                                 .rearrange("l r c -> r (l c)")).then_inc(head_in, 16)

                    def load_state(b, n):
                        po.wait_ge(s_out[b % 4], (hh * 2 + n) * 16 + 16)
                        settle(po)
                        po.dma_start(Ss[:, b % 4], st_v[one(l, 1), b, one(h, 1)]
                                     .rearrange("l h p k c -> p (l h k) c")).then_inc(s_in[b % 4], 16)

                    def store_state(b):
                        po.wait_ge(side_free, s0 + U_DS[b] + 3)
                        settle(po)
                        po.dma_start(nst_v[one(l, 1), b, one(h, 1)].rearrange("l h p k c -> p (l h k) c"),
                                     Ss[:, b % 4]).then_inc(s_out[b % 4], 16)

                    for b in range(4):
                        load_state(b, 0)
                    po.wait_ge(acc_out, l * (G_LAYER * NT) + h * (G_HEAD * NT) + 2 * NT)
                    settle(po)
                    po.dma_start(a["new_pool_prompt"][one(l, 1), 0, :, one(h * DH, DH)].rearrange("l r c -> r (l c)"),
                                 Z[P - HIST:P, NPT - 1, 0:DH]).then_inc(upool_out, 16)
                    for b in range(SB):
                        po.dma_start(a["new_pool_sample"][one(l, 1), b, :, one(h * DH, DH)]
                                     .rearrange("l r c -> r (l c)"),
                                     Z[b * SL + 1:(b + 1) * SL, NPT, 0:DH]).then_inc(upool_out, 16)
                    for b in range(4):
                        store_state(b)
                    for b in range(4, 8):
                        load_state(b, 1)
                    po.wait_ge(side_free, s0 + U_D[3] + 3)
                    settle(po)
                    po.dma_start(nsp_v[one(l, 1), 0, one(h, 1)].rearrange("l h p k c -> p (l h k) c"),
                                 Sp[:]).then_inc(sp_out, 16)
                    for b in range(4, 8):
                        store_state(b)
                    po.wait_ge(gn_in, hh + 1)
                    settle(po)
                    nc.gpsimd.tensor_tensor(gp[:], gv[:], mhalf[:], ALU.pow).then_inc(gn_pow, 1)
                po.wait_ge(side_free, l * S_LAYER + S_OUT + 2)
                settle(po)
                po.dma_start(P5[:, 0:NPT, :], a["p_prompt"][one(l, 1)].rearrange("l b (t p) c -> p (l b t) c", p=P)) \
                    .then_inc(p_in, 16)
                po.dma_start(P5[:, NPT, :], a["p_sample"][one(l, 1)].rearrange("l b s c -> (l b s) c")).then_inc(p_in, 16)
                po.wait_ge(hres_out, l * 16 + 16)
                settle(po)
                with po.Fori(0, G_OUT) as g:
                    po.wait_ge(stage_free, l * STAGES + g * NT + (HEADS * NT + 2))
                    settle(po)
                    po.dma_start(Z[:], hres_v[:, :, one(g * NW, NW)]).then_inc(res_in, 16)
                for j in range(4):
                    po.wait_ge(s_out[j], (l * HEADS + HEADS) * 32 + 16)
                settle(po)
                po.dma_start(wple, w_ple_v[one(l, 1), :, :, 0:NW].rearrange("l p k c -> p (l k) c")).then_inc(wple_in, 16)
                rsqrt(l * 2 + 2)
                with po.Fori(1, G_OUT) as g:
                    po.wait_ge(side_free, l * S_LAYER + g * PLE_UNITS + (S_PG - PLE_UNITS + 2))
                    settle(po)
                    po.dma_start(wple, w_ple_v[one(l, 1), :, :, one(g * NW, NW)].rearrange("l p k c -> p (l k) c")) \
                        .then_inc(wple_in, 16)
            po.wait_ge(h_upd, DEPTH * H_ADDS + 1)
            po.dma_start(gfin, a["g_final"].partition_broadcast(P)).then_inc(gfin_in, 16)
            rsqrt(2 * DEPTH + 1)
            po.wait_ge(upool_out, DEPTH * HEADS * 16 * (SB + 1))
            for j in range(4):
                po.wait_ge(s_out[j], DEPTH * HEADS * 32 + 16)
            po.wait_ge(sp_out, DEPTH * HEADS * 16 + 16)

        @block.scalar
        def _(ac):
            ac.sem_inc(acc_out, NT)
            ac.wait_ge(zeroed, 2)

            def hi(m0, p):
                ac.wait_ge(w_landed[p % 2], m0 * 16 + 32 * (p // 2 + 1))
                ac.wait_ge(w_used, m0 + p + 1)
                nc.scalar.activation(Whi[:, p % 2], raw[:, p % 2], ACT.Copy).then_inc(w_hi, 1)

            def t_hi(s0, ks, units, col):
                for u in units:
                    bank, unit = side[:, u % 2], T_ORDER[ks][u]
                    ac.wait_ge(side_ready, s0 + u + 1)
                    if len(unit) == 1:
                        k = unit[0]
                        last = nc.scalar.activation(Ahi[:, k, 0:NPT * P], bank, ACT.Copy,
                                                    scale=parl[:, col + k:col + k + 1])
                    else:
                        for j, k in enumerate(unit):
                            last = nc.scalar.activation(Ahi[:, k, NPT * P:TOK], bank[:, j * P:(j + 1) * P], ACT.Copy,
                                                        scale=parl[:, col + k:col + k + 1])
                    last.then_inc(t_high, 1)

            def stream(m0, jobs=lambda s: None, pairs=PAIRS):
                for s in range(KT):
                    if s % 2 == 0 and s // 2 < pairs:
                        hi(m0, s // 2 + 1)
                    jobs(s)

            def squares(n, t):
                for j in range(2):
                    if t or j:
                        ac.wait_ge(sq_done, n * (2 * NT) + 2 * t + j)
                    nc.scalar.activation(stage[:].rearrange("p a b -> p (a b)"),
                                         H[:, t, j * (D // 2):(j + 1) * (D // 2)], ACT.Square,
                                         accum_out=ssq[:, t, j:j + 1]).then_inc(sq_done, 1)

            def stage_slot(n0, t):
                ac.wait_ge(stage_free, n0 + t + (2 if t == 0 else 1))
                return stage[:, t % 2]

            def wait_acc(q, t):
                if t < NT - 1:
                    ac.wait_ge(acc_ready, q * (NT - 1) + t + 1)
                else:
                    ac.wait_ge(w_used, q * PAIRS + PAIRS + 2)

            def to_z(q):
                for t in range(NT):
                    wait_acc(q, t)
                    nc.scalar.activation(Z[:, t], acc[:, t], ACT.Copy, scale=rstd[:, t:t + 1]).then_inc(acc_out, 1)

            def to_stage(q, n0, func, scaled):
                for t in range(NT):
                    slot = stage_slot(n0, t)
                    wait_acc(q, t)
                    nc.scalar.activation(slot, acc[:, t], func, scale=rstd[:, t:t + 1] if scaled else 1.0) \
                        .then_inc(acc_out, 1)

            with ac.Fori(0, DEPTH) as l:
                def head_regs(h):
                    return (ac.snap(l * HEADS + h), ac.snap(l * M_LAYER + h * (G_HEAD * PAIRS)),
                            ac.snap(l * G_LAYER + h * G_HEAD), ac.snap(l * S_LAYER + h * H_UNITS + S_HEAD))

                def to_z_uq(h):
                    hh, m0, q0, s0 = head_regs(h)
                    ac.wait_ge(side_ready, s0)
                    to_z(q0)

                def kv_and_gates(h, extra=lambda s: None):
                    hh, m0, q0, s0 = head_regs(h)

                    def spread_q(half):
                        diag = qTm[:, half].rearrange("p b n -> p (b n)")
                        for b in range(SB):
                            last = nc.scalar.activation(
                                diag[:, b * P + b * SL:b * P + (b + 1) * SL],
                                qT[:, half, NPT * P + b * SL:NPT * P + (b + 1) * SL], ACT.Copy)
                        last.then_inc(qtm_in, 1)

                    def kv_jobs(s):
                        if s == 12:
                            ac.wait_ge(side_free, s0 + U_KT + 2)
                            spread_q(0)
                        if s == 14:
                            spread_q(1)

                    stream(m0 + PAIRS, kv_jobs)
                    ac.wait_ge(side_ready, s0 + U_KT)
                    ac.wait_ge(rot_done, hh * (2 * NT) + NT)
                    ac.wait_ge(upool_out, hh * (16 * (SB + 1)) + 16 * (SB + 1))
                    to_z(ac.snap(q0 + 1))

                    def decayed_chunk(c):
                        if c >= 2:
                            ac.wait_ge(side_ready, s0 + U_D[c - 2] + 1)
                        nc.scalar.activation(vd[:, c % 2], Z[:, c, DH:NW], ACT.Copy,
                                             scale=head[:, C_VP:C_VP + 1]).then_inc(vd_in, 1)

                    def decayed_stream(b):
                        if b >= 2:
                            ac.wait_ge(side_ready, s0 + U_DS[b - 2] + 1)
                        nc.scalar.activation(vdm[:, b % 2], Z[:, NPT, DH:NW], ACT.Copy,
                                             scale=head[:, C_VS + b:C_VS + b + 1]).then_inc(vdm_in, 1)

                    def gate_jobs(s):
                        if s == 0:
                            ac.wait_ge(head_in, hh * 48 + 48)
                            ac.wait_ge(acc_out, q0 * NT + 3 * NT)
                        for c in {0: (0, 1), 8: (2,), 11: (3,)}.get(s, ()):
                            decayed_chunk(c)
                        for b in {1: (0, 1), 8: (2, 3), 10: (4, 5), 14: (6, 7)}.get(s, ()):
                            decayed_stream(b)
                        extra(s)

                    stream(m0 + 2 * PAIRS, gate_jobs)
                    to_stage(ac.snap(q0 + 2), ac.snap(l * STAGES + h * NT), ACT.Silu, True)

                m0 = ac.snap(l * M_LAYER)
                s0 = ac.snap(l * S_LAYER)
                ac.wait_ge(parl_c, l + 1)
                hi(m0, 0)
                t_hi(s0, K_PLAIN, range(T_FIRST), PC_MIX)

                def norm_jobs(s, n, n0):
                    if s == 4:
                        ac.wait_ge(stage_free, n0 + 2)
                    if s in (5, 7, 9, 11, 12):
                        squares(n, (5, 7, 9, 11, 12).index(s))

                def first_jobs(s):
                    t_hi(s0, K_PLAIN, t_slot(s), PC_MIX)
                    norm_jobs(s, l * 2, l * STAGES)

                stream(m0, first_jobs)
                ac.wait_ge(rstd_done, l * 2 + 1)
                to_z_uq(0)
                with ac.Fori(0, HEADS - 1) as h:
                    kv_and_gates(h)
                    stream(ac.snap(l * M_LAYER + h * (G_HEAD * PAIRS) + G_HEAD * PAIRS))
                    to_z_uq(h + 1)
                s0 = ac.snap(l * S_LAYER + S_OUT)
                kv_and_gates(HEADS - 1, lambda s: t_hi(s0, K_OUT, range(T_FIRST), PC_OUT) if s == KT - 1 else None)

                m0 = ac.snap(l * M_LAYER + HEADS * G_HEAD * PAIRS)
                q0 = ac.snap(l * G_LAYER + HEADS * G_HEAD)
                n0 = ac.snap(l * STAGES + HEADS * NT)
                stream(m0, lambda s: t_hi(s0, K_OUT, t_slot(s), PC_OUT))
                to_stage(q0, n0, ACT.Copy, False)
                with ac.Fori(1, G_OUT - 1) as g:
                    stream(ac.snap(m0 + g * PAIRS))
                    to_stage(ac.snap(q0 + g), ac.snap(n0 + g * NT), ACT.Copy, False)
                s0 = ac.snap(l * S_LAYER + S_PG0)
                stream(ac.snap(m0 + (G_OUT - 1) * PAIRS),
                       lambda s: t_hi(s0, K_PLAIN, {14: (0,), 15: (1, 2)}.get(s, ()), PC_PLE))
                to_stage(ac.snap(q0 + (G_OUT - 1)), ac.snap(n0 + (G_OUT - 1) * NT), ACT.Copy, False)

                m0 = ac.snap(l * M_LAYER + (HEADS * G_HEAD + G_OUT) * PAIRS)
                q0 = ac.snap(l * G_LAYER + HEADS * G_HEAD + G_OUT)
                n0 = ac.snap(l * STAGES + (HEADS + G_OUT) * NT)

                def pg_jobs(s):
                    t_hi(s0, K_PLAIN, t_slot(s), PC_PLE)
                    norm_jobs(s, l * 2 + 1, n0)

                stream(m0, pg_jobs)
                ac.wait_ge(rstd_done, l * 2 + 2)
                to_stage(q0, n0, ACT.Sigmoid, True)
                with ac.Fori(1, G_OUT - 1) as g:
                    stream(ac.snap(m0 + g * PAIRS))
                    to_stage(ac.snap(q0 + g), ac.snap(n0 + g * NT), ACT.Sigmoid, True)
                stream(ac.snap(m0 + (G_OUT - 1) * PAIRS), pairs=PAIRS - 1)
                to_stage(ac.snap(q0 + (G_OUT - 1)), ac.snap(n0 + (G_OUT - 1) * NT), ACT.Sigmoid, True)

            ac.wait_ge(stage_free, DEPTH * STAGES + 2)
            for t in range(NT):
                ac.wait_ge(h_upd, DEPTH * H_ADDS + 1 - NT + t + 1)
                squares(2 * DEPTH, t)

        @block.vector
        def _(ve):
            ve.sem_inc(w_lo, 2)
            ve.sem_inc(side_free, 2)
            ve.sem_inc(os_free, 1)
            ve.sem_inc(stage_free, 2)
            ve.sem_inc(h_upd, 1)

            class Chain:

                def __init__(self, s, base):
                    self.s, self.base, self.n = s, base, 0

                def __call__(self, ins):
                    ins.then_inc(self.s, 1)
                    self.n += 1

                def wait(self):
                    ve.wait_ge(self.s, self.base + self.n)

            def lo(m0, p):
                ve.wait_ge(w_hi, m0 + p + 1)
                nc.vector.tensor_tensor(Wlo[:, p % 2], raw[:, p % 2], Whi[:, p % 2].bitcast(F32), ALU.subtract) \
                    .then_inc(w_lo, 1)

            def t_lo(s0, th0, ks, units, col):
                for u in units:
                    bank, unit = side[:, u % 2], T_ORDER[ks][u]
                    ve.wait_ge(t_high, th0 + u + 1)
                    for j, k in enumerate(unit):
                        tok = slice(0, NPT * P) if len(unit) == 1 else slice(NPT * P, TOK)
                        part = bank if len(unit) == 1 else bank[:, j * P:(j + 1) * P]
                        last = nc.vector.scalar_tensor_tensor(
                            out=Alo[:, k, tok], in0=part, scalar=parl[:, col + k:col + k + 1],
                            in1=Ahi[:, k, tok].bitcast(F32), op0=ALU.mult, op1=ALU.subtract)
                    last.then_inc(side_free, 1)

            def stream(m0, jobs=lambda s: None, pairs=PAIRS):
                for s in range(KT):
                    if s % 2 == 0 and s // 2 < pairs:
                        lo(m0, s // 2 + 1)
                    jobs(s)

            def mean_square(n):
                ve.wait_ge(sq_done, n * (2 * NT))
                ch = Chain(ch_ms, (n - 1) * 1)
                ch(nc.vector.tensor_tensor(ms[:], ssq[:, :, 0], ssq[:, :, 1], ALU.add))
                ch.wait()
                nc.vector.tensor_scalar(ms[:], ms[:], 1.0 / D, EPS, ALU.mult, ALU.add).then_inc(ms_done, 1)

            def rotate(ch, t, off, q):
                if ch.n:
                    ve.wait_ge(rot_done, ch.base + ch.n)
                ve.wait_ge(acc_out, q * NT + t + NT + 1)
                z = Z[:, t, off:off + DH].rearrange("p (a b) -> p a b", a=2)
                cos = rope[:, t, 0:P].unsqueeze(1).to_broadcast([P, 2, P])
                sin = rope[:, t, P:DH].unsqueeze(1).to_broadcast([P, 2, P])
                nc.vector.tensor_tensor(tA[:], z, cos, ALU.mult)
                ch(nc.vector.tensor_tensor(tB[:], z, sin, ALU.mult))
                ch.wait()
                nc.vector.tensor_tensor(z[:, 0], tA[:, 0], tB[:, 1], ALU.subtract)
                nc.vector.tensor_tensor(z[:, 1], tA[:, 1], tB[:, 0], ALU.add).then_inc(rot_done, 1)

            ve.wait_ge(par_t, 1)
            nc.vector.tensor_copy(par[:], side[:, 0, 0:DEPTH * PC_LAYER]).then_inc(par_c, 1)
            ve.wait_ge(par_c, 1)
            ve.wait_ge(const_in, 16 * (1 + 4 * DEPTH))
            for s in (*s_out, sp_out):
                ve.wait_ge(s, 16)

            with ve.Fori(0, DEPTH) as l:
                m0 = ve.snap(l * M_LAYER)
                s0 = ve.snap(l * S_LAYER)
                nc.vector.tensor_scalar(parl[:], par[:, one(l * PC_LAYER, PC_LAYER)], 1.0, None, ALU.mult) \
                    .then_inc(parl_c, 1)
                ve.wait_ge(parl_c, l + 1)
                lo(m0, 0)
                th0 = ve.snap(l * (3 * T_UNITS))
                t_lo(s0, th0, K_PLAIN, range(T_FIRST), PC_MIX)

                def first_jobs(s):
                    t_lo(s0, th0, K_PLAIN, t_slot(s), PC_MIX)
                    if s == 14:
                        mean_square(l * 2 + 1)

                stream(m0, first_jobs)

                def kv_and_gates(h, extra=lambda s: None):
                    hh = ve.snap(l * HEADS + h)
                    m0 = ve.snap(l * M_LAYER + h * (G_HEAD * PAIRS))
                    s0 = ve.snap(l * S_LAYER + h * H_UNITS + S_HEAD)
                    z0 = ve.snap(hh * (2 * NT))
                    q0 = ve.snap(l * G_LAYER + h * G_HEAD)
                    rot = Chain(ch_rot, z0)
                    ret0 = HEADS * DH

                    def evac(u, write):
                        ve.wait_ge(side_ready, s0 + u + 1)
                        write(side[:, u % 2]).then_inc(side_free, 1)

                    def copy(dst):
                        return lambda bank: nc.vector.tensor_copy(
                            dst, bank[:, 0:dst.free_size()] if len(dst.shape) == 2 else
                            bank[:, 0:dst.free_size()].rearrange("p (a b) -> p a b", a=dst.shape[1]))

                    def store_map(tiles, bank):
                        dst = H[:, tiles[0]:tiles[0] + 2, one(h * DH, DH)] if len(tiles) > 1 else \
                            H[:, tiles[0], one(h * DH, DH)]
                        src = bank.rearrange("p (t c) -> p t c", t=2) if len(tiles) > 1 else bank[:, 0:DH]
                        return nc.vector.tensor_scalar(dst, src, 1.0, None, ALU.mult)

                    def kv_jobs(s):
                        for t in {0: (0, 1), 1: (2, 3), 2: (4,)}.get(s, ()):
                            rotate(rot, t, DH, q0)
                        if s == 2:
                            evac(U_BAND, copy(pooledT[:, 0, 0:NPT * P]))
                        if s == 3:
                            evac(U_BAND + 1, copy(pooledT[:, 1, 0:NPT * P]))
                        if s == 4:
                            evac(U_BAND + 2, copy(pooledT[:, :, NPT * P:TOK]))
                            ve.wait_ge(hres_out, l * 16 + 16)
                        if s == 6:
                            evac(U_MAP, lambda bank: store_map((0, 1), bank))
                            evac(U_MAP + 1, lambda bank: store_map((2, 3), bank))
                        if s == 7:
                            evac(U_MAP + 2, lambda bank: store_map((4,), bank))
                        if s == 8:
                            evac(U_QT, copy(qT[:, 0, 0:NPT * P]))
                        if s == 9:
                            evac(U_QT + 1, copy(qT[:, 1, 0:NPT * P]))
                        if s == 10:
                            evac(U_QT + 2, copy(qT[:, :, NPT * P:TOK]))

                    stream(m0 + PAIRS, kv_jobs)

                    gn = Chain(ch_gn, hh * (2 * NT))

                    def normalize(t, bank):
                        gn(nc.vector.bn_stats(st6[:, t], bank[:, 0:DH]))
                        last = nc.vector.tensor_scalar(H[:, t, one(h * DH + ret0, DH)], bank[:, 0:DH], 1.0, None,
                                                       ALU.mult)
                        return last

                    def aggregate(t):
                        gn.wait()
                        settle(ve)
                        gn(nc.vector.bn_aggr(mv[:, t], st6[:, t]))

                    def output(c):
                        evac(U_O[c], lambda bank: normalize(c, bank))
                        aggregate(c)

                    def update(c):
                        if c == 0:
                            ve.wait_ge(sp_out, hh * 16 + 16)
                            evac(U_D[0], copy(Sp[:]))
                        else:
                            evac(U_D[c], lambda bank: nc.vector.scalar_tensor_tensor(
                                out=Sp[:].rearrange("p a b -> p (a b)"), in0=Sp[:].rearrange("p a b -> p (a b)"),
                                scalar=head[:, C_GP:C_GP + 1], in1=bank, op0=ALU.mult, op1=ALU.add))

                    def update_stream(b):
                        state = Ss[:, b % 4].rearrange("p a b -> p (a b)")
                        evac(U_DS[b], lambda bank: nc.vector.scalar_tensor_tensor(
                            out=state, in0=state, scalar=head[:, C_GS:C_GS + 1], in1=bank,
                            op0=ALU.mult, op1=ALU.add))

                    def finish_norm():
                        gn.wait()
                        gate(nc.vector.tensor_tensor(gv[:], mv[:, :, 1], head[:, C_D2:C_D2 + NT], ALU.mult))
                        gate.wait()
                        nc.vector.tensor_scalar(gv[:], gv[:], GN_EPS, None, ALU.add).then_inc(gn_in, 1)
                        ve.wait_ge(gn_pow, hh + 1)
                        gate(nc.vector.tensor_tensor(gr[:], gp[:], head[:, C_D:C_D + NT], ALU.mult))
                        gate.wait()
                        for t in range(NT):
                            o = H[:, t, one(h * DH + ret0, DH)]
                            last = nc.vector.tensor_scalar(o, o, mv[:, t, 0:1], gr[:, t:t + 1],
                                                           ALU.subtract, ALU.mult)
                        gate(last)

                    gate = Chain(ch_gate, hh * 3)

                    def gate_jobs(s):
                        for t in {0: (0, 1), 1: (2, 3), 2: (4,)}.get(s, ()):
                            rotate(rot, t, 0, q0 + 1)
                        if s == 3:
                            evac(U_KT, copy(kT[:, 0, 0:NPT * P]))
                            evac(U_KT + 1, copy(kT[:, 1, 0:NPT * P]))
                        if s == 4:
                            evac(U_KT + 2, copy(kT[:, :, NPT * P:TOK]))
                        if s == 5:
                            evac(U_SC, lambda bank: nc.vector.tensor_tensor(
                                ST[:, 0:NPT], bank.rearrange("p (c n) -> p c n", c=NPT),
                                head[:, C_MASKP:C_MASKP + P].unsqueeze(1).to_broadcast([P, NPT, P]), ALU.mult))
                        if s == 6:
                            evac(U_SC + 1, lambda bank: nc.vector.tensor_tensor(
                                ST[:, NPT], bank[:, 0:P], head[:, C_MASKS:C_MASKS + P], ALU.mult))
                            output(0)
                        if s == 7:
                            update(0)
                        for b in {8: (0, 1), 9: (2, 3)}.get(s, ()):
                            update_stream(b)
                        if s == 10:
                            output(1)
                            update(1)
                        if s == 11:
                            output(2)
                        if s == 12:
                            update(2)
                        if s == 13:
                            output(3)
                            update(3)
                            ve.wait_ge(os_ready, hh + 1)
                            normalize(NPT, osb).then_inc(os_free, 1)
                            aggregate(NPT)
                        for b in {14: (4, 5, 6), 15: (7,)}.get(s, ()):
                            update_stream(b)
                        extra(s)
                        if s == 15:
                            finish_norm()

                    stream(m0 + 2 * PAIRS, gate_jobs)
                    gate.wait()
                    for t in range(NT):
                        both = H[:, t].rearrange("p (a b) -> p a b", a=2)[:, :, one(h * DH, DH)]
                        ve.wait_ge(acc_out, q0 * NT + 2 * NT + t + NT + 1)
                        last = nc.vector.tensor_tensor(both, both, stage[:, t % 2].rearrange("p (a b) -> p a b", a=2),
                                                       ALU.mult).then_inc(stage_free, 1)
                    assert gn.n == 2 * NT and rot.n == 2 * NT and gate.n == 3

                with ve.Fori(0, HEADS - 1) as h:
                    kv_and_gates(h)
                    stream(ve.snap(l * M_LAYER + h * (G_HEAD * PAIRS) + G_HEAD * PAIRS))
                s0 = ve.snap(l * S_LAYER + S_OUT)
                th0 = ve.snap(l * (3 * T_UNITS) + T_UNITS)
                kv_and_gates(HEADS - 1,
                             lambda s: t_lo(s0, th0, K_OUT, range(T_FIRST), PC_OUT) if s == KT - 1 else None)

                m0 = ve.snap(l * M_LAYER + HEADS * G_HEAD * PAIRS)
                q0 = ve.snap(l * G_LAYER + HEADS * G_HEAD)

                def add_residual(g, q):
                    ve.wait_ge(res_in, l * (G_OUT * 16) + g * 16 + 16)
                    for t in range(NT):
                        ve.wait_ge(acc_out, q * NT + t + NT + 1)
                        nc.vector.tensor_tensor(H[:, t, one(g * NW, NW)], stage[:, t % 2], Z[:, t], ALU.add) \
                            .then_inc(stage_free, 1)

                def out_jobs(s):
                    t_lo(s0, th0, K_OUT, t_slot(s), PC_OUT)
                    for i in {12: (0, 1), 13: (2, 3)}.get(s, ()):
                        u = T_UNITS + i
                        ve.wait_ge(side_ready, s0 + u + 1)
                        dst = pT[:, i, 0:NPT * P] if i < 2 else pT[:, i - 2, NPT * P:TOK]
                        nc.vector.tensor_copy(dst, side[:, u % 2, 0:dst.free_size()]).then_inc(side_free, 1)

                stream(m0, out_jobs)
                add_residual(0, q0)
                with ve.Fori(1, G_OUT - 1) as g:
                    stream(ve.snap(m0 + g * PAIRS))
                    add_residual(g, ve.snap(q0 + g))
                s0 = ve.snap(l * S_LAYER + S_PG0)
                th0 = ve.snap(l * (3 * T_UNITS) + 2 * T_UNITS)
                stream(ve.snap(m0 + (G_OUT - 1) * PAIRS),
                       lambda s: t_lo(s0, th0, K_PLAIN, {14: (0,), 15: (1, 2)}.get(s, ()), PC_PLE))
                add_residual(G_OUT - 1, ve.snap(q0 + (G_OUT - 1)))

                m0 = ve.snap(l * M_LAYER + (HEADS * G_HEAD + G_OUT) * PAIRS)
                q0 = ve.snap(l * G_LAYER + HEADS * G_HEAD + G_OUT)

                def ple(s1, u0, i):
                    ve.wait_ge(side_ready, s1 + u0 + i + 1)
                    dst = Z[:, i] if i < NPT else Z[:, NPT, (i - NPT) * DH:(i - NPT + 1) * DH]
                    nc.vector.tensor_copy(dst, side[:, (u0 + i) % 2, 0:dst.free_size()]).then_inc(side_free, 1)

                def gate_ple(g, q):
                    ve.wait_ge(side_free, l * S_LAYER + g * PLE_UNITS + (S_PG + 2))
                    for t in range(NT):
                        ve.wait_ge(acc_out, q * NT + t + NT + 1)
                        nc.vector.tensor_tensor(Z[:, t], stage[:, t % 2], Z[:, t], ALU.mult).then_inc(stage_free, 1)

                def add_ple(g):
                    ve.wait_ge(stage_free, l * STAGES + g * NT + ((HEADS + G_OUT) * NT + NT + 2))
                    cols = H[:, :, one(g * NW, NW)]
                    nc.vector.tensor_tensor(cols, cols, Z[:], ALU.add).then_inc(h_upd, 1)

                def pg_jobs(s):
                    t_lo(s0, th0, K_PLAIN, t_slot(s), PC_PLE)
                    if 9 <= s <= 14:
                        ple(s0, T_UNITS, s - 9)
                    if s == 14:
                        mean_square(l * 2 + 2)

                def later_jobs(s, s1, g):
                    if s == 1:
                        add_ple(g - 1)
                    if s == 2:
                        ve.wait_ge(h_upd, l * H_ADDS + g + 1)
                    if s % 2 and 3 <= s <= 13:
                        ple(s1, 0, s // 2 - 1)

                stream(m0, pg_jobs)
                gate_ple(0, q0)
                with ve.Fori(1, G_OUT - 1) as g:
                    s1 = ve.snap(l * S_LAYER + g * PLE_UNITS + (S_PG - PLE_UNITS))
                    stream(ve.snap(m0 + g * PAIRS), lambda s: later_jobs(s, s1, g))
                    gate_ple(g, ve.snap(q0 + g))
                s1 = ve.snap(l * S_LAYER + S_LAYER - PLE_UNITS)
                stream(ve.snap(m0 + (G_OUT - 1) * PAIRS), lambda s: later_jobs(s, s1, G_OUT - 1), pairs=PAIRS - 1)
                gate_ple(G_OUT - 1, ve.snap(q0 + (G_OUT - 1)))
                for t in range(NT):
                    cols = H[:, t, D - NW:D]
                    ve.wait_ge(stage_free, l * STAGES + (STAGES - NT + t + 1 + 2))
                    nc.vector.tensor_tensor(cols, cols, Z[:, t], ALU.add).then_inc(h_upd, 1)

            mean_square(2 * DEPTH + 1)
            ve.wait_ge(rstd_done, 2 * DEPTH + 1)
            ve.wait_ge(gfin_in, 16)
            for t in range(NT):
                nc.vector.scalar_tensor_tensor(out=H[:, t], in0=H[:, t], scalar=rstd[:, t:t + 1], in1=gfin,
                                               op0=ALU.mult, op1=ALU.mult).then_inc(y_in, 1)

        @block.tensor
        def _(pe):
            pe.sem_inc(w_used, 2)
            pe.wait_ge(const_in, 16 * (1 + 4 * DEPTH))
            n = DEPTH * PC_LAYER
            nc.tensor.transpose(side[:, 0, 0:n], pstage, ident[0:n, 0:n]).then_inc(par_t, 1)
            pe.wait_ge(par_c, 1)

            def stream(q, ks=K_PLAIN, jobs=lambda s: None, t0=None):
                for s, k in enumerate(ks):
                    p, kk = divmod(s, 2)
                    if kk == 0:
                        pe.wait_ge(w_lo, q * PAIRS + (p + 3))
                    for t in range(NT):
                        if s == 0:
                            pe.wait_ge(acc_out, q * NT + t + 1)
                        if t0 is not None and (t == 0 or t == NPT and s in T_SAMPLE):
                            pe.wait_ge(side_free, t0 + (T_PROMPT[s] if t == 0 else T_SAMPLE[s]) + 3)
                        tok = slice(t * P, (t + 1) * P)
                        nc.tensor.matmul(acc[:, t], Ahi[:, k, tok], Whi[:, p % 2, kk], start=(s == 0), stop=False)
                        nc.tensor.matmul(acc[:, t], Ahi[:, k, tok], Wlo[:, p % 2, kk], start=False, stop=False)
                        mm = nc.tensor.matmul(acc[:, t], Alo[:, k, tok], Whi[:, p % 2, kk], start=False,
                                              stop=(s == KT - 1))
                        if kk == 1 and t == NT - 1:
                            mm.then_inc(w_used, 1)
                        elif s == KT - 1:
                            mm.then_inc(acc_ready, 1)
                    jobs(s)

            def open_unit(s0, u):
                pe.wait_ge(side_free, s0 + u + 1)
                return side[:, u % 2]

            def turn_h(s0, ks, units):
                for u in units:
                    unit = T_ORDER[ks][u]
                    bank = open_unit(s0, u)
                    for j in range(4):
                        t, k = (j, unit[0]) if len(unit) == 1 else (NPT, unit[j])
                        last = nc.tensor.transpose(bank[:, j * P:(j + 1) * P], H[:, t, k * P:(k + 1) * P], ident[:])
                    last.then_inc(side_ready, 1)

            def mm(out, lhsT, rhs, start=True, stop=True):
                return nc.tensor.matmul(out, lhsT, rhs, start=start, stop=stop)

            with pe.Fori(0, DEPTH) as l:
                s0 = pe.snap(l * S_LAYER)
                pe.wait_ge(h_upd, l * H_ADDS + 1)
                pe.wait_ge(x_in[0], 32)
                turn_h(s0, K_PLAIN, range(T_FIRST))

                def first_jobs(s):
                    for u in t_slot(s):
                        pe.wait_ge(x_in[T_ORDER[K_PLAIN][u][-1] // 4], 32)
                        turn_h(s0, K_PLAIN, (u,))

                stream(pe.snap(l * G_LAYER), jobs=first_jobs, t0=s0)

                def kv_and_gates(h, extra=lambda s: None):
                    hh = pe.snap(l * HEADS + h)
                    q0 = pe.snap(l * G_LAYER + h * G_HEAD)
                    s0 = pe.snap(l * S_LAYER + h * H_UNITS + S_HEAD)
                    z0 = pe.snap(hh * (2 * NT))

                    def band(c):
                        bank = open_unit(s0, U_BAND + c)
                        for j in range(NPT if c < 2 else 2):
                            t, ch = (j, c) if c < 2 else (NPT, j)
                            out = bank[:, j * P:(j + 1) * P]
                            cols = slice(ch * P, (ch + 1) * P)
                            if t == 0:
                                last = mm(out, Z[:, 0, cols], head[:, C_BAND0:C_BAND0 + P])
                            elif t < NPT:
                                mm(out, Z[:, t, cols], head[:, C_BAND:C_BAND + P], stop=False)
                                last = mm(out, Z[:, t - 1, cols], head[:, C_PREV:C_PREV + P], start=False)
                            else:
                                r = SB * HIST
                                mm(out, Z[:, t, cols], head[:, C_BANDS:C_BANDS + P], stop=False)
                                last = mm(out, hist[0:r, cols], head[0:r, C_HISTS:C_HISTS + P], start=False)
                        last.then_inc(side_ready, 1)

                    def pool_map(i):
                        bank = open_unit(s0, U_MAP + i)
                        for j, t in enumerate(((0, 1), (2, 3), (4,))[i]):
                            for c in range(2):
                                last = mm(bank[:, j * DH:(j + 1) * DH], pooledT[:, c, t * P:(t + 1) * P],
                                          wpool[:, c], start=(c == 0), stop=(c == 1))
                        last.then_inc(side_ready, 1)

                    def turn(u, i, off):
                        bank = open_unit(s0, u + i)
                        for j in range(NPT if i < 2 else 2):
                            t, half = (j, i) if i < 2 else (NPT, j)
                            last = nc.tensor.transpose(bank[:, j * P:(j + 1) * P],
                                                       Z[:, t, off + half * P:off + (half + 1) * P], ident[:])
                        last.then_inc(side_ready, 1)

                    def kv_jobs(s):
                        if s == 2:
                            pe.wait_ge(acc_out, q0 * NT + 2 * NT)
                            pe.wait_ge(head_in, hh * 48 + 48)
                            band(0)
                        if s == 3:
                            band(1)
                        if s == 4:
                            band(2)
                        if s == 6:
                            pe.wait_ge(side_free, s0 + U_MAP + 2)
                            pool_map(0)
                            pool_map(1)
                        if s == 7:
                            pool_map(2)
                        if 8 <= s <= 10:
                            if s == 8:
                                pe.wait_ge(rot_done, z0 + NT)
                            turn(U_QT, s - 8, DH)

                    stream(pe.snap(q0 + 1), jobs=kv_jobs)

                    def scores(u, tiles):
                        bank = open_unit(s0, u)
                        for j, t in enumerate(tiles):
                            for half in range(2):
                                last = mm(bank[:, j * P:(j + 1) * P], kT[:, half, t * P:(t + 1) * P],
                                          qT[:, half, t * P:(t + 1) * P], start=(half == 0), stop=(half == 1))
                        last.then_inc(side_ready, 1)

                    def output(c):
                        bank = open_unit(s0, U_O[c])
                        last = mm(bank[:, 0:DH], ST[:, c], Z[:, c, DH:NW], stop=(c == 0))
                        if c:
                            pe.wait_ge(side_free, s0 + U_D[c - 1] + 3)
                            for half in range(2):
                                last = mm(bank[:, 0:DH], qT[:, half, c * P:(c + 1) * P], Sp[:, half], start=False,
                                          stop=(half == 1))
                        last.then_inc(side_ready, 1)

                    def update(c):
                        bank = open_unit(s0, U_D[c])
                        pe.wait_ge(vd_in, hh * NPT + c + 1)
                        for half in range(2):
                            last = mm(bank[:, half * DH:(half + 1) * DH], Z[:, c, half * P:(half + 1) * P],
                                      vd[:, c % 2])
                        last.then_inc(side_ready, 1)

                    def stream_output(b):
                        pe.wait_ge(s_in[b % 4], hh * 32 + 16 * (b // 4 + 1))
                        for half in range(2):
                            last = mm(osb[:, 0:DH], qTm[:, half, b], Ss[:, b % 4, half], start=False,
                                      stop=(b == SB - 1 and half == 1))
                        if b == SB - 1:
                            last.then_inc(os_ready, 1)

                    def stream_update(b):
                        bank = open_unit(s0, U_DS[b])
                        pe.wait_ge(vdm_in, hh * SB + b + 1)
                        for half in range(2):
                            last = mm(bank[:, half * DH:(half + 1) * DH], Z[:, NPT, half * P:(half + 1) * P],
                                      vdm[:, b % 2])
                        last.then_inc(side_ready, 1)

                    def gate_jobs(s):
                        if s == 3:
                            pe.wait_ge(rot_done, z0 + 2 * NT)
                            turn(U_KT, 0, 0)
                            turn(U_KT, 1, 0)
                        if s == 4:
                            turn(U_KT, 2, 0)
                        if s == 5:
                            pe.wait_ge(side_free, s0 + U_KT + 4)
                            scores(U_SC, range(NPT))
                        if s == 6:
                            pe.wait_ge(side_free, s0 + U_KT + 5)
                            scores(U_SC + 1, (NPT,))
                            pe.wait_ge(side_free, s0 + U_SC + 3)
                            output(0)
                        if s == 7:
                            update(0)
                            pe.wait_ge(side_free, s0 + U_SC + 4)
                            pe.wait_ge(qtm_in, hh * 2 + 2)
                            pe.wait_ge(os_free, hh + 1)
                            mm(osb[:, 0:DH], ST[:, NPT], Z[:, NPT, DH:NW], stop=False)
                            for b in range(4):
                                stream_output(b)
                        for b in {8: (0, 1), 9: (2, 3)}.get(s, ()):
                            stream_update(b)
                        if s == 10:
                            output(1)
                            update(1)
                        if s == 11:
                            output(2)
                        if s == 12:
                            update(2)
                            for b in range(4, 8):
                                stream_output(b)
                        if s == 13:
                            output(3)
                            update(3)
                        for b in {14: (4, 5, 6), 15: (7,)}.get(s, ()):
                            stream_update(b)
                        extra(s)

                    stream(pe.snap(q0 + 2), jobs=gate_jobs)

                with pe.Fori(0, HEADS - 1) as h:
                    kv_and_gates(h)
                    stream(pe.snap(l * G_LAYER + h * G_HEAD + G_HEAD))

                def out_turns(s):
                    if s == KT - 1:
                        pe.wait_ge(stage_free, l * STAGES + ((HEADS - 1) * NT + 2))
                        turn_h(s_out0, K_OUT, range(T_FIRST))

                s_out0 = pe.snap(l * S_LAYER + S_OUT)
                kv_and_gates(HEADS - 1, out_turns)

                q0 = pe.snap(l * G_LAYER + HEADS * G_HEAD)

                def out_jobs(s):
                    for u in t_slot(s):
                        if T_ORDER[K_OUT][u][0] == K_OUT[12] and len(T_ORDER[K_OUT][u]) == 1:
                            pe.wait_ge(stage_free, l * STAGES + (HEADS * NT + 2))
                        turn_h(s_out0, K_OUT, (u,))
                    if s == 12:
                        pe.wait_ge(p_in, l * 32 + 32)
                    for i in {12: (0, 1), 13: (2, 3)}.get(s, ()):
                        bank = open_unit(s_out0, T_UNITS + i)
                        for j in range(NPT if i < 2 else 1):
                            t, half = (j, i) if i < 2 else (NPT, i - 2)
                            last = nc.tensor.transpose(bank[:, j * P:(j + 1) * P],
                                                       P5[:, t, half * P:(half + 1) * P], ident[:])
                        last.then_inc(side_ready, 1)

                stream(q0, K_OUT, out_jobs, t0=s_out0)
                with pe.Fori(1, G_OUT - 1) as g:
                    stream(pe.snap(q0 + g), K_OUT)
                s0 = pe.snap(l * S_LAYER + S_PG0)

                def next_turns(s):
                    if s == 14:
                        pe.wait_ge(stage_free, l * STAGES + ((HEADS + G_OUT - 1) * NT + 2))
                    turn_h(s0, K_PLAIN, {14: (0,), 15: (1, 2)}.get(s, ()))

                stream(pe.snap(q0 + (G_OUT - 1)), K_OUT, next_turns)

                q0 = pe.snap(l * G_LAYER + HEADS * G_HEAD + G_OUT)

                def ple(s1, u0, i):
                    bank = open_unit(s1, u0 + i)
                    t = min(i, NPT)
                    cols = slice(0, NW) if i < NPT else slice((i - NPT) * DH, (i - NPT + 1) * DH)
                    out = bank[:, 0:NW if i < NPT else DH]
                    for c in range(2):
                        last = mm(out, pT[:, c, t * P:(t + 1) * P], wple[:, c, cols], start=(c == 0), stop=(c == 1))
                    last.then_inc(side_ready, 1)

                def pg_jobs(s):
                    for u in t_slot(s):
                        if u == T_PROMPT[12]:
                            pe.wait_ge(stage_free, l * STAGES + ((HEADS + G_OUT) * NT + 2))
                        turn_h(s0, K_PLAIN, (u,))
                    if s == 9:
                        pe.wait_ge(wple_in, l * (16 * G_OUT) + 16)
                    if 9 <= s <= 14:
                        ple(s0, T_UNITS, s - 9)

                stream(q0, jobs=pg_jobs, t0=s0)

                def later_jobs(s, s1, g):
                    if s == 3:
                        pe.wait_ge(wple_in, l * (16 * G_OUT) + g * 16 + 16)
                    if s % 2 and 3 <= s <= 13:
                        ple(s1, 0, s // 2 - 1)

                with pe.Fori(1, G_OUT) as g:
                    s1 = pe.snap(l * S_LAYER + g * PLE_UNITS + (S_PG - PLE_UNITS))
                    stream(pe.snap(q0 + g), jobs=lambda s: later_jobs(s, s1, g))



_INS = ["x_prompt", "x_sample", "p_prompt", "p_sample", "state_pool", "state_ret", "g_mix", "w_in", "w_pool",
        "pool_scale", "g_gn", "w_out", "g_ple", "w_pg", "w_ple", "g_final"]
_OUTS = [("y_prompt", (1, 512, D)), ("y_sample", (SB, SL, D)),
         ("new_pool_prompt", (DEPTH, 1, HIST, HEADS * DH)), ("new_ret_prompt", (DEPTH, 1, HEADS, DH, DH)),
         ("new_pool_sample", (DEPTH, SB, HIST, HEADS * DH)), ("new_ret_sample", (DEPTH, SB, HEADS, DH, DH))]


def _tables():
    import numpy as np
    n = np.arange(P)
    pos = np.concatenate([np.arange(NPT * P), PAST + np.arange(P) % SL]).astype(np.float32)
    half = DH // 2
    inv = np.float32(1.0) / (np.float32(10000.0) ** (np.arange(half, dtype=np.float32) / np.float32(half)))
    ang = (pos[:, None] * inv[None, :].astype(np.float32)).astype(np.float32).astype(np.float64)
    rope = np.concatenate([np.cos(ang), np.sin(ang)], axis=1).reshape(NT, P, DH).transpose(1, 0, 2)

    head = np.zeros((HEADS, P, C_HEAD))
    b, i = n // SL, n % SL
    same = b[:, None] == b[None, :]
    key_scale = DH ** -0.5
    for h in range(HEADS):
        g = 1.0 - 2.0 ** (-5.0 - h)
        t = head[h]
        t[:, C_MASKP:C_MASKP + P] = (n[:, None] <= n[None, :]) * g ** -(n[:, None] + 1.0) * key_scale
        t[:, C_MASKS:C_MASKS + P] = (same & (i[:, None] <= i[None, :])) * g ** -(i[:, None] + 1.0) * key_scale
        t[:, C_D:C_D + NPT] = (g ** (n + 1.0))[:, None]
        t[:, C_D + NPT] = g ** (i + 1.0)
        t[:, C_D2:C_D2 + NT] = t[:, C_D:C_D + NT] ** 2
        t[:, C_VP] = g ** (P - 1.0 - n) * key_scale
        t[:, C_GP], t[:, C_GS] = g ** P, g ** SL
        t[:, C_VS:C_VS + SB] = (b[:, None] == np.arange(SB)) * (g ** (SL - 1.0 - i) * key_scale)[:, None]
        w = WINDOWS[h]
        inside = (n[:, None] <= n[None, :]) & (n[:, None] > n[None, :] - w)
        eye = np.eye(P)
        t[:, C_BAND0:C_BAND0 + P] = inside / np.minimum(w, n + 1.0)[None, :] - eye
        t[:, C_BAND:C_BAND + P] = inside / w - eye
        t[:, C_PREV:C_PREV + P] = (n[:, None] - P > n[None, :] - w) / w
        t[:, C_BANDS:C_BANDS + P] = (same & inside) / w - eye
        r = np.arange(SB * HIST)
        t[0:SB * HIST, C_HISTS:C_HISTS + P] = ((r // HIST)[:, None] == b[None, :]) & \
            ((r % HIST - HIST)[:, None] > i[None, :] - w)
        t[0:SB * HIST, C_HISTS:C_HISTS + P] /= w
    return {"c_ident": np.eye(P, dtype=np.float32), "c_rope": rope.astype(np.float32),
            "c_head": head.astype(np.float32)}


def kernel(**inputs):
    import numpy as _np
    import concourse.bacc as _bacc
    from concourse import mybir as _mybir
    from concourse.bass_utils import run_bass_kernel_spmd as _run

    nc = _bacc.Bacc("TRN2", target_bir_lowering=False, num_devices=1)
    arrays, a = {}, {}
    for name, value in [(n, inputs[n]) for n in _INS] + list(_tables().items()):
        value = _np.ascontiguousarray(value)
        arrays[f"in_{name}"] = value
        a[name] = nc.dram_tensor(f"in_{name}", value.shape, _mybir.dt.from_np(value.dtype), kind="ExternalInput").ap()
    for name, shape in _OUTS:
        a[name] = nc.dram_tensor(f"out_{name}", shape, F32, kind="ExternalOutput").ap()
    build(nc, a)
    r = _run(nc, [arrays], core_ids=[0])
    return tuple(r.results[0][f"out_{name}"] for name, _ in _OUTS)
```

```python
from contextlib import ExitStack

import concourse.bass as bass
from concourse import mybir

F32 = mybir.dt.float32
F32R = mybir.dt.float32r
ALU = mybir.AluOpType
ACT = mybir.ActivationFunctionType

P = 128
D = 2048
DEPTH = 2
NT = 5
TOK = NT * P
NPT = 4
SB, SL = 8, 16
HEADS = 4
DH = 256
HIST = 15
WINDOWS = (2, 4, 8, 16)
PAST = 128
PLE = 256
NW = 512
KT = D // P
PAIRS = KT // 2
EPS, GN_EPS = 1e-6, 1e-5

G_HEAD = 3
G_OUT = D // NW
G_LAYER = HEADS * G_HEAD + 2 * G_OUT
M_LAYER = G_LAYER * PAIRS

SEGMENTS = (slice(0, 3, 2), slice(3, 5), slice(1, 6, 4))

T_UNITS = 20
H_UNITS = 30
PT_UNITS = 4
PLE_UNITS = 6
S_PRO = 0
S_HEAD = S_PRO + T_UNITS
S_OUT = S_HEAD + HEADS * H_UNITS
S_PG0 = S_OUT + T_UNITS + PT_UNITS
S_PG = S_PG0 + T_UNITS + PLE_UNITS
S_LAYER = S_PG + (G_OUT - 1) * PLE_UNITS
U_BAND, U_MAP, U_QT, U_KT, U_SC = 0, 3, 6, 9, 12
U_O = (14, 20, 22, 25)
U_D = (15, 21, 23, 26)
U_DS = (16, 17, 18, 19, 24, 27, 28, 29)
SQUARES = 2 * NT + 2 * NT + 3 * NT
FINISHED = (slice(0, 1024), slice(1024, D - NW))
H_ADDS = G_OUT - 1 + NT
LAST_PLE, LAST_T = (0, 2, 4, 6, 7, 8), (1, 3, 5)
STAGES = NT * (HEADS + 2 * G_OUT)

C_MASKP, C_MASKS, C_BAND0, C_BAND, C_PREV, C_BANDS, C_HISTS = (i * P for i in range(7))
C_D = 7 * P
C_D2 = C_D + NT
C_VP = C_D2 + NT
C_GP, C_GS = C_VP + 1, C_VP + 2
C_KS = C_GS + 1
C_HEAD = C_KS + 4

SPREAD = [0]
for _b in range(SB - 1):
    SPREAD.append(SPREAD[_b] + max(P - SL * (_b + 1), SL * (_b + 1)))
SPREAD_W = SPREAD[-1] + P
STACK = 3 * SL
STACK_BASE = 64

PC_MIX, PC_OUT, PC_PLE, PC_LAYER = 0, KT, 2 * KT, 3 * KT
PARAMS = (("g_mix", PC_MIX, KT), ("pool_scale", PC_OUT, KT // 2), ("g_gn", PC_OUT + KT // 2, KT // 2),
          ("g_ple", PC_PLE, KT))

K_PLAIN = tuple(range(KT))
K_OUT = (0, 1, 2, 3, 4, 5, 8, 9, 10, 11, 12, 13, 6, 7, 14, 15)
T_ORDER = {ks: [u for i in range(KT) for u in [(ks[i],)] + ([ks[i:i + 4]] if i % 4 == 0 else [])]
           for ks in (K_PLAIN, K_OUT)}
T_PROMPT = tuple(i + (i + 3) // 4 for i in range(KT))
T_SAMPLE = {i: i + i // 4 + 1 for i in range(0, KT, 4)}
T_FIRST = 3
T_AHEAD = {4: (0,), 6: (1,), 8: (2,)}


def t_slot(s):
    return range(min(T_FIRST + 2 * s, T_UNITS), min(T_FIRST + 2 * s + 2, T_UNITS))


def next_layer(l):
    assert DEPTH == 2
    return l * -1 + (DEPTH - 1)


def build(nc, a):
    with ExitStack() as ctx:
        def sb(name, shape, dt=F32):
            return ctx.enter_context(nc.sbuf_tensor(name, shape, dt))

        def shared(first, second):
            with nc.sbuf_tensor(*first) as one_tensor:
                pass
            return one_tensor, sb(*second)

        def psum(name, shape):
            return ctx.enter_context(nc.psum_tensor(name, shape, F32))

        def sem(name):
            return ctx.enter_context(nc.semaphore(name))

        H = sb("H", [P, NT, D])
        Ahi = sb("Ahi", [P, KT, TOK], F32R)
        Alo = sb("Alo", [P, KT, TOK], F32R)
        raw = sb("raw", [P, 2, 2, NW])
        Whi = sb("Whi", [P, 2, 2, NW], F32R)
        Wlo = sb("Wlo", [P, 2, 2, NW], F32R)
        Z = sb("Z", [P, NT, NW])
        qT, pT_hi = shared(("qT", [P, 2, TOK], F32), ("pT_hi", [P, 2, TOK], F32R))
        kT, pT_lo = shared(("kT", [P, 2, TOK], F32), ("pT_lo", [P, 2, TOK], F32R))
        ST = sb("ST", [P, NT, P])
        Sp = sb("Sp", [P, 2, DH])
        vd = sb("vd", [P, 2, DH])
        P5, X = shared(("P5", [P, NT, PLE], F32), ("X", [P, 4, NW], F32R))
        qTm = sb("qTm", [P, 2, SPREAD_W])
        Ss = sb("Ss", [P, 4, 2, DH])
        head = sb("head", [P, C_HEAD])
        rope = sb("rope", [P, NT, DH])
        stage = sb("stage", [P, 2, NW])
        ident = sb("ident", [P, P])
        par = sb("par", [P, DEPTH * PC_LAYER])
        parl = sb("parl", [P, PC_LAYER])
        primer = sb("primer", [P, 1])
        ssq = sb("ssq", [P, NT, 2])
        ssq_last = sb("ssq_last", [P, NT, 3])
        ms = sb("ms", [P, NT])
        ms_last = sb("ms_last", [P, NT])
        rstd = sb("rstd", [P, NT])
        mhalf = sb("mhalf", [P, NT])
        st6 = sb("st6", [P, NT, 6])
        mv = sb("mv", [P, NT, 2])
        gv = sb("gv", [P, NT])
        gp = sb("gp", [P, NT])
        gr = sb("gr", [P, NT])

        tA, tB = ST[:, 0:2], ST[:, 2:4]
        pooledT, wpool, hist = kT, Sp, vd[:, 1]
        wple_hi, wple_lo = X[:, 0:2], X[:, 2:4]
        kv_hi, kv_lo = stage[:, 0].bitcast(F32R), stage[:, 1].bitcast(F32R)
        wple = Ss[:, 0:2].rearrange("p a b c -> p (a b c)").rearrange("p (k n) -> p k n", k=2)
        gfin_first = qTm[:].rearrange("p a n -> p (a n)")[:, 0:D - NW]
        gfin_last = Ss[:, 2].rearrange("p b c -> p (b c)")
        pstage = stage[:, 0, 0:P]

        acc = psum("acc", [P, NT, NW])
        side = psum("side", [P, 2, NW])
        osb = psum("osb", [P, NW])

        kv_parts = nc.dram_tensor("kv_parts", [P, 3, NW], F32, kind="Internal").ap()
        hres = nc.dram_tensor("h_residual", [TOK, D], F32, kind="Internal").ap()

        tables = sem("tables")
        settled = sem("settled")
        const_in = sem("const_in")
        par_t, par_c, parl_c, zeroed = sem("par_t"), sem("par_c"), sem("parl_c"), sem("zeroed")
        x_in = [sem(f"x_in{c}") for c in range(4)]
        h_upd = sem("h_upd")
        w_landed = [sem("w_landed0"), sem("w_landed1")]
        w_hi, w_lo, w_used = sem("w_hi"), sem("w_lo"), sem("w_used")
        acc_ready = sem("acc_ready")
        acc_out = sem("acc_out")
        side_ready, side_free = sem("side_ready"), sem("side_free")
        t_high = sem("t_high")
        sq_done, ms_done, rstd_done = sem("sq_done"), sem("ms_done"), sem("rstd_done")
        rot_done = sem("rot_done")
        head_in = sem("head_in")
        upool_out = sem("upool_out")
        s_in = [sem(f"s_in{j}") for j in range(4)]
        s_out = [sem(f"s_out{j}") for j in range(4)]
        sp_out = sem("sp_out")
        qtm_in, vd_in = sem("qtm_in"), sem("vd_in")
        kv_split = sem("kv_split")
        kv_written, kv_stacked = sem("kv_written"), sem("kv_stacked")
        os_ready, os_free = sem("os_ready"), sem("os_free")
        gn_in, gn_pow = sem("gn_in"), sem("gn_pow")
        stage_free = sem("stage_free")
        hres_out, res_in = sem("hres_out"), sem("res_in")
        p_in, wple_in = sem("p_in"), sem("wple_in")
        p_high, wple_high, wple_low = sem("p_high"), sem("wple_high"), sem("wple_low")
        ch_rot, ch_gn, ch_gate, ch_ms = (sem(n) for n in ("ch_rot", "ch_gn", "ch_gate", "ch_ms"))
        gfin_in, gmul_done = sem("gfin_in"), sem("gmul_done")
        y_first, y_last, y_out = sem("y_first"), sem("y_last"), sem("y_out")

        w_in_v = a["w_in"].rearrange("l (k p) (s c) -> l p k s c", p=P, s=6)
        w_out_v = a["w_out"].rearrange("l (k p) c -> l p k c", p=P)
        w_pg_v = a["w_pg"].rearrange("l (k p) c -> l p k c", p=P)
        w_ple_v = a["w_ple"].rearrange("l (k p) c -> l p k c", p=P)
        w_pool_v = a["w_pool"].rearrange("l g (k p) c -> l g p k c", p=P)
        st_v = a["state_ret"].rearrange("l b h (k p) c -> l b h p k c", p=P)
        nst_v = a["new_ret_sample"].rearrange("l b h (k p) c -> l b h p k c", p=P)
        nsp_v = a["new_ret_prompt"].rearrange("l b h (k p) c -> l b h p k c", p=P)
        hist_v = a["state_pool"].rearrange("l b j c -> l (b j) c")
        hres_v = hres.rearrange("(t p) n -> p t n", p=P)
        one = bass.ds

        block = ctx.enter_context(nc.Block())

        def settle(e):
            e.sem_inc(settled, 1)

        def load_x(e, c):
            cols = slice(c * NW, (c + 1) * NW)
            e.dma_start(H[:, 0:NPT, cols], a["x_prompt"][:, :, cols].rearrange("b (t p) n -> p (b t) n", p=P)) \
                .then_inc(x_in[c], 16)
            e.dma_start(H[:, NPT, cols], a["x_sample"][:, :, cols].rearrange("b s n -> (b s) n")) \
                .then_inc(x_in[c], 16)

        @block.sync
        def _(sp):
            load_x(sp, 0)

            def load_pair(l, h, segs, p):
                src = w_in_v[one(l, 1), :, 2 * p:2 * p + 2, segs, one(h * DH, DH)]
                for kk in range(2):
                    sp.dma_start(raw[:, p % 2, kk, :].rearrange("p (s c) -> p s c", s=2),
                                 src[:, :, kk].rearrange("l p s c -> p (l s) c")).then_inc(w_landed[p % 2], 16)

            def load_head(l, h, first=0):
                for j, segs in enumerate(SEGMENTS):
                    m0 = sp.snap(l * M_LAYER + h * (G_HEAD * PAIRS) + j * PAIRS)
                    for p in range(0 if j else first, PAIRS):
                        sp.wait_ge(w_lo, m0 + p + 1)
                        load_pair(l, h, segs, p)

            load_pair(0, 0, SEGMENTS[0], 0)
            with sp.Fori(0, DEPTH) as l:
                load_head(l, 0, first=1)
                with sp.Fori(1, HEADS) as h:
                    load_head(l, h)
                for base, view, ks in ((HEADS * G_HEAD, w_out_v, K_OUT), (HEADS * G_HEAD + G_OUT, w_pg_v, K_PLAIN)):
                    with sp.Fori(0, G_OUT) as g:
                        m0 = sp.snap(l * M_LAYER + g * PAIRS + base * PAIRS)
                        for p in range(PAIRS):
                            src = view[one(l, 1), :, ks[2 * p]:ks[2 * p] + 2, one(g * NW, NW)]
                            sp.wait_ge(w_lo, m0 + p + 1)
                            for kk in range(2):
                                sp.dma_start(raw[:, p % 2, kk, :], src[:, :, kk].rearrange("l p c -> p (l c)")) \
                                    .then_inc(w_landed[p % 2], 16)
                sp.wait_ge(w_lo, l * M_LAYER + (M_LAYER + 1))
                load_pair(sp.snap(next_layer(l)), 0, SEGMENTS[0], 0)

            for t in range(NT):
                dst = a["y_prompt"][0, t * P:(t + 1) * P, :] if t < NPT else \
                    a["y_sample"].rearrange("b s n -> (b s) n")
                for done, cols in ((y_last, slice(D - NW, D)), (y_first, slice(0, D - NW))):
                    sp.wait_ge(done, t + 1)
                    sp.dma_start(dst[:, cols], H[:, t, cols]).then_inc(y_out, 16)
            sp.wait_ge(y_out, 32 * NT)

        @block.gpsimd
        def _(po):
            po.wait_ge(const_in, 16 * (1 + len(PARAMS)))
            for c in range(1, 4):
                load_x(po, c)
            for t in range(NT):
                po.dma_start(rope[:, t], a["c_rope"][:, t]).then_inc(s_out[t] if t < 4 else sp_out, 16)
            po.memset(qTm[:], 0.0).then_inc(zeroed, 1)
            po.memset(mhalf[:], -0.5).then_inc(zeroed, 1)
            po.wait_ge(zeroed, 2)

            def rsqrt(n):
                po.wait_ge(ms_done, n)
                settle(po)
                nc.gpsimd.tensor_tensor(rstd[:], ms[:], mhalf[:], ALU.pow).then_inc(rstd_done, 1)

            with po.Fori(0, DEPTH) as l:
                for c in range(4):
                    po.wait_ge(x_in[c], 32)
                    po.wait_ge(h_upd, l * H_ADDS + (1 if c < 3 else 1 + NT))
                    settle(po)
                    cols = slice(c * NW, (c + 1) * NW)
                    po.dma_start(hres_v[:, :, cols], H[:, :, cols]).then_inc(hres_out, 16)
                rsqrt(l * 2 + 1)
                settle(po)
                with po.Fori(0, HEADS) as h:
                    hh = po.snap(l * HEADS + h)
                    s0 = po.snap(l * S_LAYER + h * H_UNITS + S_HEAD)
                    po.wait_ge(stage_free, l * STAGES + h * NT + 2)
                    settle(po)
                    po.dma_start(head[:], a["c_head"][one(h, 1)].rearrange("o p c -> p (o c)")).then_inc(head_in, 16)
                    po.wait_ge(sp_out, hh * 16 + 16)
                    settle(po)
                    po.dma_start(wpool[:], w_pool_v[one(l, 1), one(h, 1)].rearrange("l g p k c -> p (l g k) c")) \
                        .then_inc(head_in, 16)
                    po.dma_start(hist[0:SB * HIST, :], hist_v[one(l, 1), :, one(h * DH, DH)]
                                 .rearrange("l r c -> r (l c)")).then_inc(head_in, 16)

                    def load_state(b, n):
                        po.wait_ge(s_out[b % 4], (hh * 2 + n) * 16 + 16)
                        settle(po)
                        po.dma_start(Ss[:, b % 4], st_v[one(l, 1), b, one(h, 1)]
                                     .rearrange("l h p k c -> p (l h k) c")).then_inc(s_in[b % 4], 16)

                    def store_state(b):
                        po.wait_ge(side_free, s0 + U_DS[b] + 3)
                        settle(po)
                        po.dma_start(nst_v[one(l, 1), b, one(h, 1)].rearrange("l h p k c -> p (l h k) c"),
                                     Ss[:, b % 4]).then_inc(s_out[b % 4], 16)

                    for b in range(4):
                        load_state(b, 0)
                    po.wait_ge(acc_out, l * (G_LAYER * NT) + h * (G_HEAD * NT) + 2 * NT)
                    settle(po)
                    po.dma_start(a["new_pool_prompt"][one(l, 1), 0, :, one(h * DH, DH)].rearrange("l r c -> r (l c)"),
                                 Z[P - HIST:P, NPT - 1, 0:DH]).then_inc(upool_out, 16)
                    for b in range(SB):
                        po.dma_start(a["new_pool_sample"][one(l, 1), b, :, one(h * DH, DH)]
                                     .rearrange("l r c -> r (l c)"),
                                     Z[b * SL + 1:(b + 1) * SL, NPT, 0:DH]).then_inc(upool_out, 16)
                    for b in range(4):
                        store_state(b)
                    for b in range(4, 8):
                        load_state(b, 1)
                    po.wait_ge(side_free, s0 + U_D[3] + 3)
                    settle(po)
                    po.dma_start(nsp_v[one(l, 1), 0, one(h, 1)].rearrange("l h p k c -> p (l h k) c"),
                                 Sp[:]).then_inc(sp_out, 16)
                    po.wait_ge(gn_in, hh + 1)
                    settle(po)
                    nc.gpsimd.tensor_tensor(gp[:], gv[:], mhalf[:], ALU.pow).then_inc(gn_pow, 1)
                    for b in range(4, 8):
                        store_state(b)
                po.wait_ge(side_free, l * S_LAYER + S_OUT + 2)
                settle(po)
                po.dma_start(P5[:, 0:NPT, :], a["p_prompt"][one(l, 1)].rearrange("l b (t p) c -> p (l b t) c", p=P)) \
                    .then_inc(p_in, 16)
                po.dma_start(P5[:, NPT, :], a["p_sample"][one(l, 1)].rearrange("l b s c -> (l b s) c")) \
                    .then_inc(p_in, 16)
                po.wait_ge(hres_out, l * 64 + 64)
                settle(po)
                with po.Fori(0, G_OUT) as g:
                    po.wait_ge(stage_free, l * STAGES + g * NT + (HEADS * NT + 2))
                    settle(po)
                    po.dma_start(Z[:], hres_v[:, :, one(g * NW, NW)]).then_inc(res_in, 16)
                for j in range(4):
                    po.wait_ge(s_out[j], (l * HEADS + HEADS) * 32 + 16)
                settle(po)
                po.dma_start(wple, w_ple_v[one(l, 1), :, :, 0:NW].rearrange("l p k c -> p (l k) c")) \
                    .then_inc(wple_in, 16)
                rsqrt(l * 2 + 2)
                with po.Fori(1, G_OUT) as g:
                    po.wait_ge(wple_low, l * G_OUT + g)
                    settle(po)
                    po.dma_start(wple, w_ple_v[one(l, 1), :, :, one(g * NW, NW)].rearrange("l p k c -> p (l k) c")) \
                        .then_inc(wple_in, 16)
            po.wait_ge(os_ready, DEPTH * HEADS)
            for dst, cols in ((gfin_first, slice(0, D - NW)), (gfin_last, slice(D - NW, D))):
                po.dma_start(dst, a["g_final"][cols].partition_broadcast(P)).then_inc(gfin_in, 16)
            po.wait_ge(gfin_in, 32)
            po.wait_ge(side_ready, DEPTH * S_LAYER - PLE_UNITS + LAST_T[-1] + 1)
            cols = slice(0, D - NW)
            for t in range(NT):
                po.wait_ge(sq_done, DEPTH * SQUARES - 3 * NT + 2 * t + 2)
                nc.gpsimd.tensor_tensor(H[:, t, cols], H[:, t, cols], gfin_first, ALU.mult).then_inc(gmul_done, 1)
            for t in range(NT):
                po.wait_ge(ms_done, 2 * DEPTH + t + 1)
                nc.gpsimd.tensor_tensor(rstd[:, t:t + 1], ms[:, t:t + 1], mhalf[:, t:t + 1], ALU.pow) \
                    .then_inc(rstd_done, 1)
            po.wait_ge(upool_out, DEPTH * HEADS * 16 * (SB + 1))
            for j in range(4):
                po.wait_ge(s_out[j], DEPTH * HEADS * 32 + 16)
            po.wait_ge(sp_out, DEPTH * HEADS * 16 + 16)

        @block.scalar
        def _(ac):
            ac.sem_inc(acc_out, NT)
            ac.sem_inc(kv_stacked, 32)

            def load_table(n, func):
                ac.wait_ge(tables, n)
                nc.scalar.activation(primer[:], primer[:], func).then_inc(tables, 1)

            ac.dma_start(ident[:], a["c_ident"]).then_inc(const_in, 16)
            for name, col, n in PARAMS:
                ac.dma_start(pstage[DEPTH * col:DEPTH * (col + n)],
                             a[name].rearrange("l (k c) -> (l k) c", c=P)).then_inc(const_in, 16)
            load_table(1, ACT.Sigmoid)

            def hi(m0, p):
                ac.wait_ge(w_landed[p % 2], m0 * 16 + 32 * (p // 2 + 1))
                ac.wait_ge(w_used, m0 + p + 1)
                nc.scalar.activation(Whi[:, p % 2], raw[:, p % 2], ACT.Copy).then_inc(w_hi, 1)

            def t_hi(s0, ks, units, col, numbers=range(T_UNITS)):
                for u in units:
                    bank, unit = side[:, numbers[u] % 2], T_ORDER[ks][u]
                    ac.wait_ge(side_ready, s0 + numbers[u] + 1)
                    if len(unit) == 1:
                        k = unit[0]
                        last = nc.scalar.activation(Ahi[:, k, 0:NPT * P], bank, ACT.Copy,
                                                    scale=parl[:, col + k:col + k + 1])
                    else:
                        for j, k in enumerate(unit):
                            last = nc.scalar.activation(Ahi[:, k, NPT * P:TOK], bank[:, j * P:(j + 1) * P], ACT.Copy,
                                                        scale=parl[:, col + k:col + k + 1])
                    last.then_inc(t_high, 1)

            def stream(m0, jobs=lambda s: None, pairs=PAIRS):
                for s in range(KT):
                    if s % 2 == 0 and s // 2 < pairs:
                        hi(m0, s // 2 + 1)
                    jobs(s)

            def square(base, i, cols, total):
                if i:
                    ac.wait_ge(sq_done, base + i)
                t, c = i // 2, cols.stop - cols.start
                nc.scalar.activation(stage[:].rearrange("p a b -> p (a b)")[:, 0:c], H[:, t, cols], ACT.Square,
                                     accum_out=total).then_inc(sq_done, 1)

            def squares(base, t):
                for j in range(2):
                    square(base, 2 * t + j, slice(j * (D // 2), (j + 1) * (D // 2)), ssq[:, t, j:j + 1])

            def stage_slot(n0, t):
                ac.wait_ge(stage_free, n0 + t + (2 if t == 0 else 1))
                return stage[:, t % 2]

            def wait_acc(q, t):
                if t < NT - 1:
                    ac.wait_ge(acc_ready, q * (NT - 1) + t + 1)
                else:
                    ac.wait_ge(w_used, q * PAIRS + PAIRS + 2)

            def to_z(q):
                for t in range(NT):
                    wait_acc(q, t)
                    nc.scalar.activation(Z[:, t], acc[:, t], ACT.Copy, scale=rstd[:, t:t + 1]).then_inc(acc_out, 1)

            def to_stage_tile(q, n0, func, scaled, t):
                slot = stage_slot(n0, t)
                wait_acc(q, t)
                nc.scalar.activation(slot, acc[:, t], func, scale=rstd[:, t:t + 1] if scaled else 1.0) \
                    .then_inc(acc_out, 1)

            def to_stage(q, n0, func, scaled):
                for t in range(NT):
                    to_stage_tile(q, n0, func, scaled, t)

            ac.wait_ge(parl_c, 1)
            t_hi(0, K_PLAIN, (0,), PC_MIX)
            hi(0, 0)
            t_hi(0, K_PLAIN, (1, 2), PC_MIX)

            with ac.Fori(0, DEPTH) as l:
                def head_regs(h):
                    return (ac.snap(l * HEADS + h), ac.snap(l * M_LAYER + h * (G_HEAD * PAIRS)),
                            ac.snap(l * G_LAYER + h * G_HEAD), ac.snap(l * S_LAYER + h * H_UNITS + S_HEAD))

                def to_z_uq(h):
                    hh, m0, q0, s0 = head_regs(h)
                    ac.wait_ge(side_ready, s0)
                    to_z(q0)

                def kv_and_gates(h, extra=lambda s: None):
                    hh, m0, q0, s0 = head_regs(h)

                    def spread_q(half):
                        for b in range(SB):
                            last = nc.scalar.activation(
                                qTm[:, half, SPREAD[b] + b * SL:SPREAD[b] + (b + 1) * SL],
                                qT[:, half, NPT * P + b * SL:NPT * P + (b + 1) * SL], ACT.Copy)
                        last.then_inc(qtm_in, 1)

                    def kv_jobs(s):
                        if s == 12:
                            ac.wait_ge(zeroed, 2)
                            ac.wait_ge(side_free, s0 + U_KT + 2)
                            spread_q(0)
                        if s == 14:
                            spread_q(1)

                    stream(m0 + PAIRS, kv_jobs)
                    ac.wait_ge(side_ready, s0 + U_KT)
                    ac.wait_ge(rot_done, hh * (2 * NT) + NT)
                    ac.wait_ge(upool_out, hh * (16 * (SB + 1)) + 16 * (SB + 1))
                    to_z(ac.snap(q0 + 1))

                    def decayed_chunk(c):
                        if c >= 2:
                            ac.wait_ge(side_ready, s0 + U_D[c - 2] + 1)
                        nc.scalar.activation(vd[:, c % 2], Z[:, c, DH:NW], ACT.Copy,
                                             scale=head[:, C_VP:C_VP + 1]).then_inc(vd_in, 1)

                    def split_kv():
                        ac.wait_ge(rot_done, hh * (2 * NT) + 2 * NT)
                        ac.wait_ge(stage_free, l * STAGES + h * NT + 2)
                        nc.scalar.activation(kv_hi[:, 0:DH], Z[:, NPT, 0:DH], ACT.Copy, scale=head[:, C_KS:C_KS + 1])
                        nc.scalar.activation(kv_hi[:, DH:NW], Z[:, NPT, DH:NW], ACT.Copy).then_inc(kv_split, 1)

                    def write_kv():
                        ac.wait_ge(kv_split, hh * 2 + 2)
                        ac.wait_ge(kv_stacked, hh * 32 + 32)
                        k, v = slice(0, DH), slice(DH, NW)
                        for dst, part, cols in ((slice(0, 2), 0, k), (slice(0, 3, 2), 0, v),
                                                (slice(1, 2), 1, v), (slice(2, 3), 1, k)):
                            n = len(range(*dst.indices(3)))
                            ac.dma_start(kv_parts[:, dst, cols],
                                         stage[:, part, cols].unsqueeze(1).to_broadcast([P, n, DH])) \
                                .then_inc(kv_written, 16)

                    def stack_kv():
                        ac.wait_ge(kv_written, hh * 64 + 64)
                        ac.wait_ge(side_ready, s0 + U_SC)
                        for i in range(2):
                            ac.dma_start(X[i * STACK_BASE:i * STACK_BASE + STACK].bitcast(F32),
                                         kv_parts[i * (P // 2):(i + 1) * (P // 2)]
                                         .rearrange("(b j) i c -> (j i) b c", j=SL)).then_inc(kv_stacked, 16)

                    def gate_jobs(s):
                        if s == 0:
                            ac.wait_ge(head_in, hh * 48 + 48)
                            ac.wait_ge(acc_out, q0 * NT + 3 * NT)
                        for c in {0: (0, 1), 8: (2,), 11: (3,)}.get(s, ()):
                            decayed_chunk(c)
                        if s in (3, 4, 6):
                            {3: split_kv, 4: write_kv, 6: stack_kv}[s]()
                        extra(s)

                    stream(m0 + 2 * PAIRS, gate_jobs)
                    to_stage(ac.snap(q0 + 2), ac.snap(l * STAGES + h * NT), ACT.Silu, True)

                m0 = ac.snap(l * M_LAYER)
                s0 = ac.snap(l * S_LAYER)

                def norm_jobs(s, base, n0):
                    if s == 4:
                        ac.wait_ge(stage_free, n0 + 2)
                    if s in (6, 8, 10, 12, 13):
                        squares(base, (6, 8, 10, 12, 13).index(s))

                def first_jobs(s):
                    t_hi(s0, K_PLAIN, t_slot(s), PC_MIX)
                    if s == 6:
                        ac.wait_ge(h_upd, l * H_ADDS + 1 + NT)
                    norm_jobs(s, l * SQUARES, l * STAGES)
                    if s == 15:
                        load_table(l * 2 + 2, ACT.Silu)

                stream(m0, first_jobs)
                ac.wait_ge(rstd_done, l * 2 + 1)
                to_z_uq(0)
                with ac.Fori(0, HEADS - 1) as h:
                    kv_and_gates(h)
                    stream(ac.snap(l * M_LAYER + h * (G_HEAD * PAIRS) + G_HEAD * PAIRS))
                    to_z_uq(h + 1)
                s0 = ac.snap(l * S_LAYER + S_OUT)
                kv_and_gates(HEADS - 1, lambda s: t_hi(s0, K_OUT, {14: (0, 1, 2)}.get(s, ()), PC_OUT))

                m0 = ac.snap(l * M_LAYER + HEADS * G_HEAD * PAIRS)
                q0 = ac.snap(l * G_LAYER + HEADS * G_HEAD)
                n0 = ac.snap(l * STAGES + HEADS * NT)
                stream(m0, lambda s: t_hi(s0, K_OUT, t_slot(s), PC_OUT))
                to_stage(q0, n0, ACT.Copy, False)
                with ac.Fori(1, G_OUT - 1) as g:
                    stream(ac.snap(m0 + g * PAIRS))
                    to_stage(ac.snap(q0 + g), ac.snap(n0 + g * NT), ACT.Copy, False)
                s0 = ac.snap(l * S_LAYER + S_PG0)
                stream(ac.snap(m0 + (G_OUT - 1) * PAIRS),
                       lambda s: t_hi(s0, K_PLAIN, {12: (0,), 13: (1,), 14: (2,)}.get(s, ()), PC_PLE))
                to_stage(ac.snap(q0 + (G_OUT - 1)), ac.snap(n0 + (G_OUT - 1) * NT), ACT.Copy, False)

                m0 = ac.snap(l * M_LAYER + (HEADS * G_HEAD + G_OUT) * PAIRS)
                q0 = ac.snap(l * G_LAYER + HEADS * G_HEAD + G_OUT)
                n0 = ac.snap(l * STAGES + (HEADS + G_OUT) * NT)

                def split_wple(g, n):
                    ac.wait_ge(wple_in, l * (16 * G_OUT) + g * 16 + 16)
                    ac.wait_ge(side_ready, n)
                    nc.scalar.activation(wple_hi, wple, ACT.Copy).then_inc(wple_high, 1)

                def later_jobs(s, g):
                    if s == 0:
                        split_wple(g, l * S_LAYER + g * PLE_UNITS + (S_PG - PLE_UNITS))

                def pg_jobs(s):
                    t_hi(s0, K_PLAIN, t_slot(s), PC_PLE)
                    if s == 6:
                        split_wple(0, s0)
                    norm_jobs(s, l * SQUARES + 2 * NT, n0)
                    if s == 15:
                        load_table(l * 2 + 3, ACT.Sigmoid)

                stream(m0, pg_jobs)
                ac.wait_ge(rstd_done, l * 2 + 2)
                to_stage(q0, n0, ACT.Sigmoid, True)
                with ac.Fori(1, G_OUT - 1) as g:
                    stream(ac.snap(m0 + g * PAIRS), lambda s: later_jobs(s, g))
                    to_stage(ac.snap(q0 + g), ac.snap(n0 + g * NT), ACT.Sigmoid, True)

                def finished_jobs(s):
                    later_jobs(s, G_OUT - 1)
                    if s == 1:
                        ac.wait_ge(h_upd, l * H_ADDS + (G_OUT - 1) + (1 + NT))
                        ac.wait_ge(stage_free, n0 + ((G_OUT - 1) * NT + 2))
                    if 1 <= s <= 2 * NT:
                        t, j = divmod(s - 1, 2)
                        square(l * SQUARES + 4 * NT, s - 1, FINISHED[j], ssq_last[:, t, j:j + 1])
                    if s == 4:
                        ac.wait_ge(parl_c, l + 2)
                    t_hi(s_last, K_PLAIN, T_AHEAD.get(s, ()), PC_MIX, LAST_T)

                s_last = ac.snap(l * S_LAYER + (S_LAYER - PLE_UNITS))
                stream(ac.snap(m0 + (G_OUT - 1) * PAIRS), finished_jobs)
                ac.wait_ge(sq_done, l * SQUARES + 6 * NT)

                def square_last(t):
                    ac.wait_ge(h_upd, l * H_ADDS + (G_OUT - 1) + (1 + NT) + t + 1)
                    nc.scalar.activation(Z[:, t], H[:, t, D - NW:D], ACT.Square,
                                         accum_out=ssq_last[:, t, 2:3]).then_inc(sq_done, 1)

                for t in range(NT):
                    to_stage_tile(ac.snap(q0 + (G_OUT - 1)), ac.snap(n0 + (G_OUT - 1) * NT), ACT.Sigmoid, True, t)
                    if t:
                        square_last(t - 1)
                square_last(NT - 1)

            for t in range(NT):
                ac.wait_ge(gmul_done, t + 1)
                ac.wait_ge(rstd_done, 2 * DEPTH + t + 1)
                cols = slice(0, D - NW)
                nc.scalar.activation(H[:, t, cols], H[:, t, cols], ACT.Copy, scale=rstd[:, t:t + 1]) \
                    .then_inc(y_first, 1)

        @block.vector
        def _(ve):
            ve.sem_inc(w_lo, 2)
            ve.sem_inc(side_free, 2)
            ve.sem_inc(os_free, 1)
            ve.sem_inc(stage_free, 2)
            ve.sem_inc(h_upd, 1 + NT)
            nc.vector.memset(primer[:], 0.0).then_inc(tables, 1)

            class Chain:

                def __init__(self, s, base):
                    self.s, self.base, self.n = s, base, 0

                def __call__(self, ins):
                    ins.then_inc(self.s, 1)
                    self.n += 1

                def wait(self):
                    ve.wait_ge(self.s, self.base + self.n)

            def lo(m0, p):
                ve.wait_ge(w_hi, m0 + p + 1)
                nc.vector.tensor_tensor(Wlo[:, p % 2], raw[:, p % 2], Whi[:, p % 2].bitcast(F32), ALU.subtract) \
                    .then_inc(w_lo, 1)

            def t_lo(th0, ks, units, col, numbers=range(T_UNITS)):
                for u in units:
                    bank, unit = side[:, numbers[u] % 2], T_ORDER[ks][u]
                    ve.wait_ge(t_high, th0 + u + 1)
                    for j, k in enumerate(unit):
                        tok = slice(0, NPT * P) if len(unit) == 1 else slice(NPT * P, TOK)
                        part = bank if len(unit) == 1 else bank[:, j * P:(j + 1) * P]
                        last = nc.vector.scalar_tensor_tensor(
                            out=Alo[:, k, tok], in0=part, scalar=parl[:, col + k:col + k + 1],
                            in1=Ahi[:, k, tok].bitcast(F32), op0=ALU.mult, op1=ALU.subtract)
                    last.then_inc(side_free, 1)

            def stream(m0, jobs=lambda s: None, pairs=PAIRS):
                for s in range(KT):
                    if s % 2 == 0 and s // 2 < pairs:
                        lo(m0, s // 2 + 1)
                    jobs(s)

            def mean_square(l, i):
                ve.wait_ge(sq_done, l * SQUARES + (i + 1) * (2 * NT))
                ch = Chain(ch_ms, l * 2 + i)
                ch(nc.vector.tensor_tensor(ms[:], ssq[:, :, 0], ssq[:, :, 1], ALU.add))
                ch.wait()
                nc.vector.tensor_scalar(ms[:], ms[:], 1.0 / D, EPS, ALU.mult, ALU.add).then_inc(ms_done, 1)

            def rotate(ch, t, off, q):
                if ch.n:
                    ve.wait_ge(rot_done, ch.base + ch.n)
                ve.wait_ge(acc_out, q * NT + t + NT + 1)
                z = Z[:, t, off:off + DH].rearrange("p (a b) -> p a b", a=2)
                cos = rope[:, t, 0:P].unsqueeze(1).to_broadcast([P, 2, P])
                sin = rope[:, t, P:DH].unsqueeze(1).to_broadcast([P, 2, P])
                nc.vector.tensor_tensor(tA, z, cos, ALU.mult)
                ch(nc.vector.tensor_tensor(tB, z, sin, ALU.mult))
                ch.wait()
                nc.vector.tensor_tensor(z[:, 0], tA[:, 0], tB[:, 1], ALU.subtract)
                nc.vector.tensor_tensor(z[:, 1], tA[:, 1], tB[:, 0], ALU.add).then_inc(rot_done, 1)

            ve.wait_ge(par_t, 1)
            for _, col, n in PARAMS:
                src = side[:, 0, DEPTH * col:DEPTH * (col + n)].rearrange("p (l k) -> p l k", l=DEPTH)
                nc.vector.tensor_copy(par[:].rearrange("p (l k) -> p l k", l=DEPTH)[:, :, col:col + n], src) \
                    .then_inc(par_c, 1)
            ve.wait_ge(par_c, len(PARAMS))

            nc.vector.tensor_copy(parl[:], par[:, 0:PC_LAYER]).then_inc(parl_c, 1)
            ve.wait_ge(parl_c, 1)
            t_lo(0, K_PLAIN, (0,), PC_MIX)
            lo(0, 0)
            t_lo(0, K_PLAIN, (1, 2), PC_MIX)

            with ve.Fori(0, DEPTH) as l:
                m0 = ve.snap(l * M_LAYER)
                th0 = ve.snap(l * (3 * T_UNITS))

                def first_jobs(s):
                    t_lo(th0, K_PLAIN, t_slot(s), PC_MIX)
                    if s == 15:
                        mean_square(l, 0)

                stream(m0, first_jobs)
                for s in (*s_out, sp_out):
                    ve.wait_ge(s, 16)

                def kv_and_gates(h, extra=lambda s: None):
                    hh = ve.snap(l * HEADS + h)
                    m0 = ve.snap(l * M_LAYER + h * (G_HEAD * PAIRS))
                    s0 = ve.snap(l * S_LAYER + h * H_UNITS + S_HEAD)
                    z0 = ve.snap(hh * (2 * NT))
                    q0 = ve.snap(l * G_LAYER + h * G_HEAD)
                    rot = Chain(ch_rot, z0)
                    ret0 = HEADS * DH

                    def evac(u, write):
                        ve.wait_ge(side_ready, s0 + u + 1)
                        write(side[:, u % 2]).then_inc(side_free, 1)

                    def copy(dst):
                        return lambda bank: nc.vector.tensor_copy(
                            dst, bank[:, 0:dst.free_size()] if len(dst.shape) == 2 else
                            bank[:, 0:dst.free_size()].rearrange("p (a b) -> p a b", a=dst.shape[1]))

                    def store_map(tiles, bank):
                        dst = H[:, tiles[0]:tiles[0] + 2, one(h * DH, DH)] if len(tiles) > 1 else \
                            H[:, tiles[0], one(h * DH, DH)]
                        src = bank.rearrange("p (t c) -> p t c", t=2) if len(tiles) > 1 else bank[:, 0:DH]
                        return nc.vector.tensor_scalar(dst, src, 1.0, None, ALU.mult)

                    def kv_jobs(s):
                        for t in {0: (0, 1), 1: (2, 3), 2: (4,)}.get(s, ()):
                            rotate(rot, t, DH, q0)
                        if s == 2:
                            evac(U_BAND, copy(pooledT[:, 0, 0:NPT * P]))
                        if s == 3:
                            evac(U_BAND + 1, copy(pooledT[:, 1, 0:NPT * P]))
                        if s == 4:
                            evac(U_BAND + 2, copy(pooledT[:, :, NPT * P:TOK]))
                            ve.wait_ge(hres_out, l * 64 + 64)
                        if s == 6:
                            evac(U_MAP, lambda bank: store_map((0, 1), bank))
                            evac(U_MAP + 1, lambda bank: store_map((2, 3), bank))
                        if s == 7:
                            evac(U_MAP + 2, lambda bank: store_map((4,), bank))
                        if s == 8:
                            evac(U_QT, copy(qT[:, 0, 0:NPT * P]))
                        if s == 9:
                            evac(U_QT + 1, copy(qT[:, 1, 0:NPT * P]))
                        if s == 10:
                            evac(U_QT + 2, copy(qT[:, :, NPT * P:TOK]))

                    stream(m0 + PAIRS, kv_jobs)

                    gn = Chain(ch_gn, hh * (2 * NT))

                    def normalize(t, bank):
                        gn(nc.vector.bn_stats(st6[:, t], bank[:, 0:DH]))
                        last = nc.vector.tensor_scalar(H[:, t, one(h * DH + ret0, DH)], bank[:, 0:DH], 1.0, None,
                                                       ALU.mult)
                        return last

                    def aggregate(t):
                        gn.wait()
                        settle(ve)
                        gn(nc.vector.bn_aggr(mv[:, t], st6[:, t]))

                    def output(c):
                        evac(U_O[c], lambda bank: normalize(c, bank))
                        aggregate(c)

                    def update(c):
                        if c == 0:
                            ve.wait_ge(sp_out, hh * 16 + 16)
                            evac(U_D[0], copy(Sp[:]))
                        else:
                            evac(U_D[c], lambda bank: nc.vector.scalar_tensor_tensor(
                                out=Sp[:].rearrange("p a b -> p (a b)"), in0=Sp[:].rearrange("p a b -> p (a b)"),
                                scalar=head[:, C_GP:C_GP + 1], in1=bank, op0=ALU.mult, op1=ALU.add))

                    def update_stream(b):
                        state = Ss[:, b % 4].rearrange("p a b -> p (a b)")
                        evac(U_DS[b], lambda bank: nc.vector.scalar_tensor_tensor(
                            out=state, in0=state, scalar=head[:, C_GS:C_GS + 1], in1=bank,
                            op0=ALU.mult, op1=ALU.add))

                    def row_variance():
                        gn.wait()
                        gate(nc.vector.tensor_tensor(gv[:], mv[:, :, 1], head[:, C_D2:C_D2 + NT], ALU.mult))
                        gate.wait()
                        nc.vector.tensor_scalar(gv[:], gv[:], GN_EPS, None, ALU.add).then_inc(gn_in, 1)

                    def finish_norm():
                        ve.wait_ge(gn_pow, hh + 1)
                        gate(nc.vector.tensor_tensor(gr[:], gp[:], head[:, C_D:C_D + NT], ALU.mult))
                        gate.wait()
                        for t in range(NT):
                            o = H[:, t, one(h * DH + ret0, DH)]
                            last = nc.vector.tensor_scalar(o, o, mv[:, t, 0:1], gr[:, t:t + 1],
                                                           ALU.subtract, ALU.mult)
                        gate(last)

                    gate = Chain(ch_gate, hh * 3)

                    def gate_jobs(s):
                        for t in {0: (0, 1), 1: (2, 3), 2: (4,)}.get(s, ()):
                            rotate(rot, t, 0, q0 + 1)
                        if s == 3:
                            evac(U_KT, copy(kT[:, 0, 0:NPT * P]))
                            evac(U_KT + 1, copy(kT[:, 1, 0:NPT * P]))
                        if s == 4:
                            evac(U_KT + 2, copy(kT[:, :, NPT * P:TOK]))
                            ve.wait_ge(kv_split, hh * 2 + 1)
                            ve.wait_ge(stage_free, l * STAGES + h * NT + 2)
                            nc.vector.scalar_tensor_tensor(
                                out=kv_lo[:, 0:DH], in0=Z[:, NPT, 0:DH], scalar=head[:, C_KS:C_KS + 1],
                                in1=kv_hi[:, 0:DH].bitcast(F32), op0=ALU.mult, op1=ALU.subtract)
                            nc.vector.tensor_tensor(kv_lo[:, DH:NW], Z[:, NPT, DH:NW],
                                                    kv_hi[:, DH:NW].bitcast(F32), ALU.subtract).then_inc(kv_split, 1)
                        if s == 5:
                            ve.wait_ge(rot_done, z0 + 2 * NT)
                            evac(U_SC, lambda bank: nc.vector.tensor_tensor(
                                ST[:, 0:NPT], bank.rearrange("p (c n) -> p c n", c=NPT),
                                head[:, C_MASKP:C_MASKP + P].unsqueeze(1).to_broadcast([P, NPT, P]), ALU.mult))
                        if s == 6:
                            evac(U_SC + 1, lambda bank: nc.vector.tensor_tensor(
                                ST[:, NPT], bank[:, 0:P], head[:, C_MASKS:C_MASKS + P], ALU.mult))
                            output(0)
                        if s == 7:
                            update(0)
                        for b in {8: (0, 1), 9: (2, 3)}.get(s, ()):
                            update_stream(b)
                        if s == 10:
                            output(1)
                            update(1)
                        if s == 11:
                            output(2)
                        if s == 12:
                            update(2)
                        if s == 13:
                            output(3)
                            update(3)
                            ve.wait_ge(os_ready, hh + 1)
                            normalize(NPT, osb).then_inc(os_free, 1)
                            aggregate(NPT)
                        if s == 14:
                            row_variance()
                        for b in {12: (4,), 13: (5,), 14: (6, 7)}.get(s, ()):
                            update_stream(b)
                        if s == 15:
                            finish_norm()
                        extra(s)

                    stream(m0 + 2 * PAIRS, gate_jobs)
                    gate.wait()
                    for t in range(NT):
                        both = H[:, t].rearrange("p (a b) -> p a b", a=2)[:, :, one(h * DH, DH)]
                        ve.wait_ge(acc_out, q0 * NT + 2 * NT + t + NT + 1)
                        last = nc.vector.tensor_tensor(both, both, stage[:, t % 2].rearrange("p (a b) -> p a b", a=2),
                                                       ALU.mult).then_inc(stage_free, 1)
                    assert gn.n == 2 * NT and rot.n == 2 * NT and gate.n == 3

                with ve.Fori(0, HEADS - 1) as h:
                    kv_and_gates(h)
                    stream(ve.snap(l * M_LAYER + h * (G_HEAD * PAIRS) + G_HEAD * PAIRS))
                s0 = ve.snap(l * S_LAYER + S_OUT)
                th0 = ve.snap(l * (3 * T_UNITS) + T_UNITS)
                kv_and_gates(HEADS - 1,
                             lambda s: t_lo(th0, K_OUT, {14: (0, 1, 2)}.get(s, ()), PC_OUT))

                m0 = ve.snap(l * M_LAYER + HEADS * G_HEAD * PAIRS)
                q0 = ve.snap(l * G_LAYER + HEADS * G_HEAD)

                def add_residual(g, q):
                    ve.wait_ge(res_in, l * (G_OUT * 16) + g * 16 + 16)
                    for t in range(NT):
                        ve.wait_ge(acc_out, q * NT + t + NT + 1)
                        nc.vector.tensor_tensor(H[:, t, one(g * NW, NW)], stage[:, t % 2], Z[:, t], ALU.add) \
                            .then_inc(stage_free, 1)

                def out_jobs(s):
                    t_lo(th0, K_OUT, t_slot(s), PC_OUT)
                    for i in {12: (0, 1), 13: (2, 3)}.get(s, ()):
                        u = T_UNITS + i
                        ve.wait_ge(side_ready, s0 + u + 1)
                        c, tok = (i, slice(0, NPT * P)) if i < 2 else (i - 2, slice(NPT * P, TOK))
                        bank = side[:, u % 2, 0:tok.stop - tok.start]
                        nc.vector.tensor_copy(pT_hi[:, c, tok], bank).then_inc(p_high, 1)
                        ve.wait_ge(p_high, l * PT_UNITS + i + 1)
                        nc.vector.tensor_tensor(pT_lo[:, c, tok], bank, pT_hi[:, c, tok].bitcast(F32), ALU.subtract) \
                            .then_inc(side_free, 1)

                stream(m0, out_jobs)
                add_residual(0, q0)
                with ve.Fori(1, G_OUT - 1) as g:
                    stream(ve.snap(m0 + g * PAIRS))
                    add_residual(g, ve.snap(q0 + g))
                s0 = ve.snap(l * S_LAYER + S_PG0)
                th0 = ve.snap(l * (3 * T_UNITS) + 2 * T_UNITS)
                stream(ve.snap(m0 + (G_OUT - 1) * PAIRS),
                       lambda s: t_lo(th0, K_PLAIN, {12: (0,), 13: (1,), 14: (2,)}.get(s, ()), PC_PLE))
                add_residual(G_OUT - 1, ve.snap(q0 + (G_OUT - 1)))

                m0 = ve.snap(l * M_LAYER + (HEADS * G_HEAD + G_OUT) * PAIRS)
                q0 = ve.snap(l * G_LAYER + HEADS * G_HEAD + G_OUT)

                def ple(s1, u, i):
                    ve.wait_ge(side_ready, s1 + u + 1)
                    dst = Z[:, i] if i < NPT else Z[:, NPT, (i - NPT) * DH:(i - NPT + 1) * DH]
                    nc.vector.tensor_copy(dst, side[:, u % 2, 0:dst.free_size()]).then_inc(side_free, 1)

                def gate_ple(g, q):
                    ve.wait_ge(side_free, l * S_LAYER + g * PLE_UNITS + (S_PG + 2))
                    for t in range(NT):
                        ve.wait_ge(acc_out, q * NT + t + NT + 1)
                        nc.vector.tensor_tensor(Z[:, t], stage[:, t % 2], Z[:, t], ALU.mult).then_inc(stage_free, 1)

                def add_ple(g):
                    ve.wait_ge(stage_free, l * STAGES + g * NT + ((HEADS + G_OUT) * NT + NT + 2))
                    cols = H[:, :, one(g * NW, NW)]
                    nc.vector.tensor_tensor(cols, cols, Z[:], ALU.add).then_inc(h_upd, 1)

                def split_wple(g):
                    ve.wait_ge(wple_high, l * G_OUT + g + 1)
                    nc.vector.tensor_tensor(wple_lo, wple, wple_hi.bitcast(F32), ALU.subtract).then_inc(wple_low, 1)

                def pg_jobs(s):
                    t_lo(th0, K_PLAIN, t_slot(s), PC_PLE)
                    if s == 7:
                        split_wple(0)
                    if 9 <= s <= 14:
                        ple(s0, T_UNITS + s - 9, s - 9)
                    if s == 14:
                        mean_square(l, 1)

                def later_jobs(s, s1, g, numbers=range(PLE_UNITS)):
                    if s == 1:
                        split_wple(g)
                        add_ple(g - 1)
                    if s == 2:
                        ve.wait_ge(h_upd, l * H_ADDS + g + (1 + NT))
                    if s % 2 and 3 <= s <= 13:
                        ple(s1, numbers[s // 2 - 1], s // 2 - 1)

                stream(m0, pg_jobs)
                gate_ple(0, q0)
                with ve.Fori(1, G_OUT - 1) as g:
                    s1 = ve.snap(l * S_LAYER + g * PLE_UNITS + (S_PG - PLE_UNITS))
                    stream(ve.snap(m0 + g * PAIRS), lambda s: later_jobs(s, s1, g))
                    gate_ple(g, ve.snap(q0 + g))
                s1 = ve.snap(l * S_LAYER + S_LAYER - PLE_UNITS)
                th1 = ve.snap(l * (3 * T_UNITS) + 3 * T_UNITS)

                def last_jobs(s):
                    later_jobs(s, s1, G_OUT - 1, LAST_PLE)
                    if s == 2:
                        nc.vector.tensor_scalar(parl[:], par[:, one(next_layer(l) * PC_LAYER, PC_LAYER)], 1.0, None,
                                                ALU.mult).then_inc(parl_c, 1)
                        ve.wait_ge(parl_c, l + 2)
                    t_lo(th1, K_PLAIN, T_AHEAD.get(s, ()), PC_MIX, LAST_T)

                stream(ve.snap(m0 + (G_OUT - 1) * PAIRS), last_jobs)
                ve.wait_ge(side_free, l * S_LAYER + (S_LAYER + T_FIRST + 2))
                for t in range(NT):
                    ve.wait_ge(acc_out, l * (G_LAYER * NT) + (G_LAYER * NT + t + 1))
                    nc.vector.tensor_tensor(Z[:, t], stage[:, t % 2], Z[:, t], ALU.mult).then_inc(stage_free, 1)
                    ve.wait_ge(stage_free, l * STAGES + (STAGES - NT + t + 1 + 2))
                    cols = H[:, t, D - NW:D]
                    nc.vector.tensor_tensor(cols, cols, Z[:, t], ALU.add).then_inc(h_upd, 1)

            ve.wait_ge(sq_done, DEPTH * SQUARES - NT)
            ch = Chain(ch_ms, 2 * DEPTH)
            ch(nc.vector.tensor_tensor(ms_last[:], ssq_last[:, :, 0], ssq_last[:, :, 1], ALU.add))
            ch.wait()
            ch(nc.vector.tensor_scalar(ms_last[:], ms_last[:], 1.0 / D, EPS, ALU.mult, ALU.add))
            ch.wait()
            ve.wait_ge(gfin_in, 32)

            def mean_of_tile(t):
                ve.wait_ge(sq_done, DEPTH * SQUARES - NT + t + 1)
                nc.vector.scalar_tensor_tensor(out=ms[:, t:t + 1], in0=ssq_last[:, t, 2:3], scalar=1.0 / D,
                                               in1=ms_last[:, t:t + 1], op0=ALU.mult, op1=ALU.add) \
                    .then_inc(ms_done, 1)

            def finish_tile(t):
                ve.wait_ge(rstd_done, 2 * DEPTH + t + 1)
                cols = slice(D - NW, D)
                nc.vector.scalar_tensor_tensor(out=H[:, t, cols], in0=H[:, t, cols], scalar=rstd[:, t:t + 1],
                                               in1=gfin_last, op0=ALU.mult, op1=ALU.mult).then_inc(y_last, 1)

            for t in range(NT):
                mean_of_tile(t)
            for t in range(NT):
                finish_tile(t)

        @block.tensor
        def _(pe):
            pe.sem_inc(w_used, 2)
            pe.wait_ge(const_in, 16 * (1 + len(PARAMS)))
            n = DEPTH * PC_LAYER
            nc.tensor.transpose(side[:, 0, 0:n], pstage[0:n], ident[0:n, 0:n]).then_inc(par_t, 1)
            pe.wait_ge(par_c, len(PARAMS))

            def stream(q, ks=K_PLAIN, jobs=lambda s: None, t0=None, by_tiles=False):
                def tile(s, t):
                    k = ks[s]
                    p, kk = divmod(s, 2)
                    if s == 0:
                        pe.wait_ge(acc_out, q * NT + t + 1)
                    if t0 is not None and (t == 0 or t == NPT and s in T_SAMPLE):
                        pe.wait_ge(side_free, t0 + (T_PROMPT[s] if t == 0 else T_SAMPLE[s]) + 3)
                    tok = slice(t * P, (t + 1) * P)
                    nc.tensor.matmul(acc[:, t], Ahi[:, k, tok], Whi[:, p % 2, kk], start=(s == 0), stop=False)
                    nc.tensor.matmul(acc[:, t], Ahi[:, k, tok], Wlo[:, p % 2, kk], start=False, stop=False)
                    mm = nc.tensor.matmul(acc[:, t], Alo[:, k, tok], Whi[:, p % 2, kk], start=False,
                                          stop=(s == KT - 1))
                    if kk == 1 and t == NT - 1:
                        mm.then_inc(w_used, 1)
                    elif s == KT - 1:
                        mm.then_inc(acc_ready, 1)

                for s in range(KT - (2 if by_tiles else 0)):
                    if s % 2 == 0:
                        pe.wait_ge(w_lo, q * PAIRS + (s // 2 + 3))
                    for t in range(NT):
                        tile(s, t)
                    jobs(s)
                if by_tiles:
                    pe.wait_ge(w_lo, q * PAIRS + PAIRS + 2)
                    for t in range(NT):
                        tile(KT - 2, t)
                        tile(KT - 1, t)

            def open_unit(s0, u):
                pe.wait_ge(side_free, s0 + u + 1)
                return side[:, u % 2]

            def turn_h(s0, ks, units, numbers=range(T_UNITS)):
                for u in units:
                    unit = T_ORDER[ks][u]
                    bank = open_unit(s0, numbers[u])
                    for j in range(4):
                        t, k = (j, unit[0]) if len(unit) == 1 else (NPT, unit[j])
                        last = nc.tensor.transpose(bank[:, j * P:(j + 1) * P], H[:, t, k * P:(k + 1) * P], ident[:])
                    last.then_inc(side_ready, 1)

            def mm(out, lhsT, rhs, start=True, stop=True):
                return nc.tensor.matmul(out, lhsT, rhs, start=start, stop=stop)

            pe.wait_ge(x_in[0], 32)
            turn_h(0, K_PLAIN, range(T_FIRST))

            with pe.Fori(0, DEPTH) as l:
                s0 = pe.snap(l * S_LAYER)
                pe.wait_ge(h_upd, l * H_ADDS + 1)

                def first_jobs(s):
                    for u in t_slot(s):
                        pe.wait_ge(x_in[T_ORDER[K_PLAIN][u][-1] // 4], 32)
                        if u == T_PROMPT[12]:
                            pe.wait_ge(h_upd, l * H_ADDS + 1 + NT)
                        turn_h(s0, K_PLAIN, (u,))

                stream(pe.snap(l * G_LAYER), jobs=first_jobs, t0=s0)

                def kv_and_gates(h, extra=lambda s: None):
                    hh = pe.snap(l * HEADS + h)
                    q0 = pe.snap(l * G_LAYER + h * G_HEAD)
                    s0 = pe.snap(l * S_LAYER + h * H_UNITS + S_HEAD)
                    z0 = pe.snap(hh * (2 * NT))

                    def band(c):
                        bank = open_unit(s0, U_BAND + c)
                        for j in range(NPT if c < 2 else 2):
                            t, ch = (j, c) if c < 2 else (NPT, j)
                            out = bank[:, j * P:(j + 1) * P]
                            cols = slice(ch * P, (ch + 1) * P)
                            if t == 0:
                                last = mm(out, Z[:, 0, cols], head[:, C_BAND0:C_BAND0 + P])
                            elif t < NPT:
                                mm(out, Z[:, t, cols], head[:, C_BAND:C_BAND + P], stop=False)
                                last = mm(out, Z[:, t - 1, cols], head[:, C_PREV:C_PREV + P], start=False)
                            else:
                                r = SB * HIST
                                mm(out, Z[:, t, cols], head[:, C_BANDS:C_BANDS + P], stop=False)
                                last = mm(out, hist[0:r, cols], head[0:r, C_HISTS:C_HISTS + P], start=False)
                        last.then_inc(side_ready, 1)

                    def pool_map(i):
                        bank = open_unit(s0, U_MAP + i)
                        for j, t in enumerate(((0, 1), (2, 3), (4,))[i]):
                            for c in range(2):
                                last = mm(bank[:, j * DH:(j + 1) * DH], pooledT[:, c, t * P:(t + 1) * P],
                                          wpool[:, c], start=(c == 0), stop=(c == 1))
                        last.then_inc(side_ready, 1)

                    def turn(u, i, off):
                        bank = open_unit(s0, u + i)
                        for j in range(NPT if i < 2 else 2):
                            t, half = (j, i) if i < 2 else (NPT, j)
                            last = nc.tensor.transpose(bank[:, j * P:(j + 1) * P],
                                                       Z[:, t, off + half * P:off + (half + 1) * P], ident[:])
                        last.then_inc(side_ready, 1)

                    def kv_jobs(s):
                        if s == 2:
                            pe.wait_ge(acc_out, q0 * NT + 2 * NT)
                            pe.wait_ge(head_in, hh * 48 + 48)
                            band(0)
                        if s == 3:
                            band(1)
                        if s == 4:
                            band(2)
                        if s == 6:
                            pe.wait_ge(side_free, s0 + U_MAP + 2)
                            pool_map(0)
                            pool_map(1)
                        if s == 7:
                            pool_map(2)
                        if 8 <= s <= 10:
                            if s == 8:
                                pe.wait_ge(rot_done, z0 + NT)
                            turn(U_QT, s - 8, DH)

                    stream(pe.snap(q0 + 1), jobs=kv_jobs)

                    def scores(u, tiles):
                        bank = open_unit(s0, u)
                        for j, t in enumerate(tiles):
                            for half in range(2):
                                last = mm(bank[:, j * P:(j + 1) * P], kT[:, half, t * P:(t + 1) * P],
                                          qT[:, half, t * P:(t + 1) * P], start=(half == 0), stop=(half == 1))
                        last.then_inc(side_ready, 1)

                    def output(c):
                        bank = open_unit(s0, U_O[c])
                        last = mm(bank[:, 0:DH], ST[:, c], Z[:, c, DH:NW], stop=(c == 0))
                        if c:
                            pe.wait_ge(side_free, s0 + U_D[c - 1] + 3)
                            for half in range(2):
                                last = mm(bank[:, 0:DH], qT[:, half, c * P:(c + 1) * P], Sp[:, half], start=False,
                                          stop=(half == 1))
                        last.then_inc(side_ready, 1)

                    def update(c):
                        bank = open_unit(s0, U_D[c])
                        pe.wait_ge(vd_in, hh * NPT + c + 1)
                        for half in range(2):
                            last = mm(bank[:, half * DH:(half + 1) * DH], Z[:, c, half * P:(half + 1) * P],
                                      vd[:, c % 2])
                        last.then_inc(side_ready, 1)

                    def stream_output(b):
                        pe.wait_ge(s_in[b % 4], hh * 32 + 16 * (b // 4 + 1))
                        for half in range(2):
                            last = mm(osb[:, 0:DH], qTm[:, half, SPREAD[b]:SPREAD[b] + P], Ss[:, b % 4, half],
                                      start=False, stop=(b == SB - 1 and half == 1))
                        if b == SB - 1:
                            last.then_inc(os_ready, 1)

                    def stream_update(b):
                        bank = open_unit(s0, U_DS[b])
                        if b == 0:
                            pe.wait_ge(kv_stacked, hh * 32 + 64)
                        block_rows = slice(b // 4 * STACK_BASE, b // 4 * STACK_BASE + STACK)
                        kv = X[block_rows, b % 4]
                        for half in range(2):
                            last = mm(bank[:, half * DH:(half + 1) * DH], kv[:, half * P:(half + 1) * P], kv[:, DH:NW])
                        last.then_inc(side_ready, 1)

                    def gate_jobs(s):
                        if s == 3:
                            pe.wait_ge(rot_done, z0 + 2 * NT)
                            turn(U_KT, 0, 0)
                            turn(U_KT, 1, 0)
                        if s == 4:
                            turn(U_KT, 2, 0)
                        if s == 5:
                            pe.wait_ge(side_free, s0 + U_KT + 4)
                            scores(U_SC, range(NPT))
                        if s == 6:
                            pe.wait_ge(side_free, s0 + U_KT + 5)
                            scores(U_SC + 1, (NPT,))
                            pe.wait_ge(side_free, s0 + U_SC + 3)
                            output(0)
                        if s == 7:
                            update(0)
                            pe.wait_ge(side_free, s0 + U_SC + 4)
                            pe.wait_ge(qtm_in, hh * 2 + 2)
                            pe.wait_ge(os_free, hh + 1)
                            mm(osb[:, 0:DH], ST[:, NPT], Z[:, NPT, DH:NW], stop=False)
                            for b in range(4):
                                stream_output(b)
                        for b in {8: (0, 1), 9: (2, 3)}.get(s, ()):
                            stream_update(b)
                        if s == 10:
                            output(1)
                            update(1)
                        if s == 11:
                            output(2)
                        if s == 12:
                            update(2)
                            for b in range(4, 8):
                                stream_output(b)
                            stream_update(4)
                        if s == 13:
                            output(3)
                            update(3)
                        for b in {13: (5,), 14: (6, 7)}.get(s, ()):
                            stream_update(b)
                        extra(s)

                    stream(pe.snap(q0 + 2), jobs=gate_jobs)

                with pe.Fori(0, HEADS - 1) as h:
                    kv_and_gates(h)
                    stream(pe.snap(l * G_LAYER + h * G_HEAD + G_HEAD))

                def out_turns(s):
                    if s == 14:
                        pe.wait_ge(stage_free, l * STAGES + ((HEADS - 1) * NT + 2))
                    turn_h(s_out0, K_OUT, {14: (0, 1, 2)}.get(s, ()))

                s_out0 = pe.snap(l * S_LAYER + S_OUT)
                kv_and_gates(HEADS - 1, out_turns)

                q0 = pe.snap(l * G_LAYER + HEADS * G_HEAD)

                def out_jobs(s):
                    for u in t_slot(s):
                        if T_ORDER[K_OUT][u][0] == K_OUT[12] and len(T_ORDER[K_OUT][u]) == 1:
                            pe.wait_ge(stage_free, l * STAGES + (HEADS * NT + 2))
                        turn_h(s_out0, K_OUT, (u,))
                    if s == 12:
                        pe.wait_ge(p_in, l * 32 + 32)
                    for i in {12: (0, 1), 13: (2, 3)}.get(s, ()):
                        bank = open_unit(s_out0, T_UNITS + i)
                        for j in range(NPT if i < 2 else 1):
                            t, half = (j, i) if i < 2 else (NPT, i - 2)
                            last = nc.tensor.transpose(bank[:, j * P:(j + 1) * P],
                                                       P5[:, t, half * P:(half + 1) * P], ident[:])
                        last.then_inc(side_ready, 1)

                stream(q0, K_OUT, out_jobs, t0=s_out0)
                with pe.Fori(1, G_OUT - 1) as g:
                    stream(pe.snap(q0 + g), K_OUT)
                s0 = pe.snap(l * S_LAYER + S_PG0)

                def next_turns(s):
                    if s == 12:
                        pe.wait_ge(stage_free, l * STAGES + ((HEADS + G_OUT - 1) * NT + 2))
                    turn_h(s0, K_PLAIN, {12: (0,), 13: (1,), 14: (2,)}.get(s, ()))

                stream(pe.snap(q0 + (G_OUT - 1)), K_OUT, next_turns)

                q0 = pe.snap(l * G_LAYER + HEADS * G_HEAD + G_OUT)

                def ple(s1, u, i):
                    bank = open_unit(s1, u)
                    t = min(i, NPT)
                    cols = slice(0, NW) if i < NPT else slice((i - NPT) * DH, (i - NPT + 1) * DH)
                    out = bank[:, 0:NW if i < NPT else DH]
                    for c in range(2):
                        tok = slice(t * P, (t + 1) * P)
                        mm(out, pT_hi[:, c, tok], wple_hi[:, c, cols], start=(c == 0), stop=False)
                        mm(out, pT_hi[:, c, tok], wple_lo[:, c, cols], start=False, stop=False)
                        last = mm(out, pT_lo[:, c, tok], wple_hi[:, c, cols], start=False, stop=(c == 1))
                    last.then_inc(side_ready, 1)

                def pg_jobs(s):
                    for u in t_slot(s):
                        if u == T_PROMPT[12]:
                            pe.wait_ge(stage_free, l * STAGES + ((HEADS + G_OUT) * NT + 2))
                        turn_h(s0, K_PLAIN, (u,))
                    if s == 9:
                        pe.wait_ge(wple_low, l * G_OUT + 1)
                    if 9 <= s <= 14:
                        ple(s0, T_UNITS + s - 9, s - 9)

                stream(q0, jobs=pg_jobs, t0=s0)

                def later_jobs(s, s1, g, numbers=range(PLE_UNITS)):
                    if s == 3:
                        pe.wait_ge(wple_low, l * G_OUT + g + 1)
                    if s % 2 and 3 <= s <= 13:
                        ple(s1, numbers[s // 2 - 1], s // 2 - 1)

                with pe.Fori(1, G_OUT - 1) as g:
                    s1 = pe.snap(l * S_LAYER + g * PLE_UNITS + (S_PG - PLE_UNITS))
                    stream(pe.snap(q0 + g), jobs=lambda s: later_jobs(s, s1, g))
                s1 = pe.snap(l * S_LAYER + S_LAYER - PLE_UNITS)

                def last_jobs(s):
                    later_jobs(s, s1, G_OUT - 1, LAST_PLE)
                    if s == 4:
                        pe.wait_ge(h_upd, l * H_ADDS + (2 + NT))
                    turn_h(s1, K_PLAIN, T_AHEAD.get(s, ()), LAST_T)

                stream(pe.snap(q0 + (G_OUT - 1)), jobs=last_jobs, by_tiles=True)



_INS = ["x_prompt", "x_sample", "p_prompt", "p_sample", "state_pool", "state_ret", "g_mix", "w_in", "w_pool",
        "pool_scale", "g_gn", "w_out", "g_ple", "w_pg", "w_ple", "g_final"]
_OUTS = [("y_prompt", (1, 512, D)), ("y_sample", (SB, SL, D)),
         ("new_pool_prompt", (DEPTH, 1, HIST, HEADS * DH)), ("new_ret_prompt", (DEPTH, 1, HEADS, DH, DH)),
         ("new_pool_sample", (DEPTH, SB, HIST, HEADS * DH)), ("new_ret_sample", (DEPTH, SB, HEADS, DH, DH))]


def _tables():
    import numpy as np
    n = np.arange(P)
    pos = np.concatenate([np.arange(NPT * P), PAST + np.arange(P) % SL]).astype(np.float32)
    half = DH // 2
    inv = np.float32(1.0) / (np.float32(10000.0) ** (np.arange(half, dtype=np.float32) / np.float32(half)))
    ang = (pos[:, None] * inv[None, :].astype(np.float32)).astype(np.float32).astype(np.float64)
    rope = np.concatenate([np.cos(ang), np.sin(ang)], axis=1).reshape(NT, P, DH).transpose(1, 0, 2)

    head = np.zeros((HEADS, P, C_HEAD))
    b, i = n // SL, n % SL
    same = b[:, None] == b[None, :]
    key_scale = DH ** -0.5
    for h in range(HEADS):
        g = 1.0 - 2.0 ** (-5.0 - h)
        t = head[h]
        t[:, C_MASKP:C_MASKP + P] = (n[:, None] <= n[None, :]) * g ** -(n[:, None] + 1.0) * key_scale
        t[:, C_MASKS:C_MASKS + P] = (same & (i[:, None] <= i[None, :])) * g ** -(i[:, None] + 1.0) * key_scale
        t[:, C_D:C_D + NPT] = (g ** (n + 1.0))[:, None]
        t[:, C_D + NPT] = g ** (i + 1.0)
        t[:, C_D2:C_D2 + NT] = t[:, C_D:C_D + NT] ** 2
        t[:, C_VP] = g ** (P - 1.0 - n) * key_scale
        t[:, C_GP], t[:, C_GS] = g ** P, g ** SL
        t[:, C_KS] = g ** (SL - 1.0 - i) * key_scale
        w = WINDOWS[h]
        inside = (n[:, None] <= n[None, :]) & (n[:, None] > n[None, :] - w)
        eye = np.eye(P)
        t[:, C_BAND0:C_BAND0 + P] = inside / np.minimum(w, n + 1.0)[None, :] - eye
        t[:, C_BAND:C_BAND + P] = inside / w - eye
        t[:, C_PREV:C_PREV + P] = (n[:, None] - P > n[None, :] - w) / w
        t[:, C_BANDS:C_BANDS + P] = (same & inside) / w - eye
        r = np.arange(SB * HIST)
        t[0:SB * HIST, C_HISTS:C_HISTS + P] = ((r // HIST)[:, None] == b[None, :]) & \
            ((r % HIST - HIST)[:, None] > i[None, :] - w)
        t[0:SB * HIST, C_HISTS:C_HISTS + P] /= w
    return {"c_ident": np.eye(P, dtype=np.float32), "c_rope": rope.astype(np.float32),
            "c_head": head.astype(np.float32)}


def kernel(**inputs):
    import numpy as _np
    import concourse.bacc as _bacc
    from concourse import mybir as _mybir
    from concourse.bass_utils import run_bass_kernel_spmd as _run

    nc = _bacc.Bacc("TRN2", target_bir_lowering=False, num_devices=1)
    arrays, a = {}, {}
    for name, value in [(n, inputs[n]) for n in _INS] + list(_tables().items()):
        value = _np.ascontiguousarray(value)
        arrays[f"in_{name}"] = value
        a[name] = nc.dram_tensor(f"in_{name}", value.shape, _mybir.dt.from_np(value.dtype), kind="ExternalInput").ap()
    for name, shape in _OUTS:
        a[name] = nc.dram_tensor(f"out_{name}", shape, F32, kind="ExternalOutput").ap()
    build(nc, a)
    r = _run(nc, [arrays], core_ids=[0])
    return tuple(r.results[0][f"out_{name}"] for name, _ in _OUTS)
```
